# Optimizing a Trainium2 kernel written in Bass

```python
import jax, jax.numpy as jnp
from jax import lax
import numpy as np

D_MODEL = 1024
BATCH = 1
SEQ = 1024
DEPTH = 2
DEC_BATCH = 8
DEC_SEQ = 1
PAST_LEN = 1024
PAGE_SIZE = 128

N_EVEN = (DEPTH + 1) // 2
N_ODD = DEPTH // 2
H_RET = 4
DK_RET = 128
DV_RET = 128
RET_CHUNK = 128
ROPE_BASE = 10000.0
H_SB = 4
HD_SB = 128
SB_BLOCK = 128
CONV_W = 31
D_FF = 2816
FFN_CONV_W = 3
N_MEM = 256
H_X = 4
HD_X = D_MODEL // H_X
NORM_EPS = 1e-6
W_RK = H_RET * DK_RET
W_RV = H_RET * DV_RET
W_SB = H_SB * HD_SB
D_IN_AB = 2 * W_RK + 2 * W_RV + 3 * W_SB
D_OUT_AB = W_RV + W_SB
SPLIT_AB = [int(s) for s in np.cumsum([W_RK, W_RK, W_RV, W_RV, W_SB, W_SB])]

kernel_name = "retnet_stickbreak_conformer_hybrid_step"

def rmsnorm(x, g):
    xf = x.astype(jnp.float32)
    return (xf * lax.rsqrt(jnp.mean(xf * xf, -1, keepdims=True) + NORM_EPS) * g).astype(x.dtype)

def layernorm(x, g, b):
    xf = x.astype(jnp.float32)
    mu = jnp.mean(xf, -1, keepdims=True)
    var = jnp.mean(jnp.square(xf - mu), -1, keepdims=True)
    return ((xf - mu) * lax.rsqrt(var + NORM_EPS) * g + b).astype(x.dtype)

def rotary(x, pos):
    half = x.shape[-1] // 2
    inv = ROPE_BASE ** (-jnp.arange(half, dtype=jnp.float32) / half)
    ang = pos.astype(jnp.float32)[:, None] * inv[None, :]
    cos = jnp.cos(ang)[None, :, None, :]
    sin = jnp.sin(ang)[None, :, None, :]
    xf = x.astype(jnp.float32)
    x1, x2 = xf[..., :half], xf[..., half:]
    return jnp.concatenate([x1 * cos - x2 * sin, x1 * sin + x2 * cos], -1)

def retention_chunk(q, k, v, s0, log_gamma):
    c = q.shape[1]
    idx = jnp.arange(c)
    diff = idx[:, None] - idx[None, :]
    expo = jnp.maximum(diff, 0).astype(jnp.float32)[None] * log_gamma[:, None, None]
    dmask = jnp.where(diff[None] >= 0, jnp.exp(expo), 0.0)
    scores = jnp.einsum('bchd,bshd->bhcs', q, k) * dmask[None]
    intra = jnp.einsum('bhcs,bshe->bche', scores, v)
    q_decay = jnp.exp((idx + 1).astype(jnp.float32)[:, None] * log_gamma[None, :])
    inter = jnp.einsum('bchd,bhde->bche', q, s0) * q_decay[None, :, :, None]
    k_decay = jnp.exp((c - 1 - idx).astype(jnp.float32)[:, None] * log_gamma[None, :])
    s1 = (jnp.exp(c * log_gamma)[None, :, None, None] * s0
          + jnp.einsum('bchd,bche->bhde', k * k_decay[None, :, :, None], v))
    return intra + inter, s1

def retention_prompt(q, k, v, log_gamma):
    b, t, h, dk = q.shape
    nc = t // RET_CHUNK
    def chunks(a):
        return a.reshape(b, nc, RET_CHUNK, h, a.shape[-1]).swapaxes(0, 1)
    s0 = jnp.zeros((b, h, dk, v.shape[-1]), jnp.float32)
    def step(s, qkv):
        o, s_new = retention_chunk(qkv[0], qkv[1], qkv[2], s, log_gamma)
        return s_new, o
    s_end, o = lax.scan(step, s0, (chunks(q), chunks(k), chunks(v)))
    return o.swapaxes(0, 1).reshape(b, t, h, v.shape[-1]), s_end

def head_layernorm(o, g):
    mu = jnp.mean(o, -1, keepdims=True)
    var = jnp.mean(jnp.square(o - mu), -1, keepdims=True)
    on = (o - mu) * lax.rsqrt(var + NORM_EPS)
    return on.reshape(o.shape[0], o.shape[1], -1) * g

def sb_attend(q, qpos, k, v, kpos, bias):
    z = (jnp.einsum('bqhd,bkhd->bhqk', q, k).astype(jnp.float32) * (HD_SB ** -0.5)
         + bias.astype(jnp.float32)[None, :, None, None])
    mask = kpos[None, :] < qpos[:, None]
    log_1m = jnp.where(mask, jax.nn.log_sigmoid(-z), 0.0)
    after = lax.cumsum(log_1m, axis=3, reverse=True) - log_1m
    a = jnp.where(mask, jnp.exp(jax.nn.log_sigmoid(z) + after), 0.0)
    return jnp.einsum('bhqk,bkhd->bqhd', a.astype(v.dtype), v)

def sb_prompt(q, k, v, bias):
    b, t, h, d = q.shape
    nb = t // SB_BLOCK
    qb = q.reshape(b, nb, SB_BLOCK, h, d).swapaxes(0, 1)
    kpos = jnp.arange(t)
    def block(args):
        qi, i = args
        return sb_attend(qi, i * SB_BLOCK + jnp.arange(SB_BLOCK), k, v, kpos, bias)
    o = lax.map(block, (qb, jnp.arange(nb)))
    return o.swapaxes(0, 1).reshape(b, t, h, d)

def gather_pages(cache_l, page_table):
    g = cache_l[page_table]
    return g.reshape(page_table.shape[0], -1, cache_l.shape[2], cache_l.shape[3])

def mixer_ab(h, pos, s_ret, past_k, past_v, w_in, gn_g, w_out, sb_bias, log_gamma):
    b, t, _ = h.shape
    rq, rk, rv, rg, sq, sk, sv = jnp.split(h @ w_in, SPLIT_AB, axis=-1)
    q = rotary(rq.reshape(b, t, H_RET, DK_RET), pos)
    k = rotary(rk.reshape(b, t, H_RET, DK_RET), pos) * (DK_RET ** -0.5)
    v = rv.reshape(b, t, H_RET, DV_RET).astype(jnp.float32)
    if s_ret is None:
        o, s_new = retention_prompt(q, k, v, log_gamma)
    else:
        o, s_new = retention_chunk(q, k, v, s_ret.astype(jnp.float32), log_gamma)
    ret_out = jax.nn.silu(rg.astype(jnp.float32)) * head_layernorm(o, gn_g)
    qs = sq.reshape(b, t, H_SB, HD_SB)
    ks = sk.reshape(b, t, H_SB, HD_SB)
    vs = sv.reshape(b, t, H_SB, HD_SB)
    if past_k is None:
        sb = sb_prompt(qs, ks, vs, sb_bias)
    else:
        k_all = jnp.concatenate([past_k.astype(ks.dtype), ks], axis=1)
        v_all = jnp.concatenate([past_v.astype(vs.dtype), vs], axis=1)
        sb = sb_attend(qs, pos, k_all, v_all, jnp.arange(k_all.shape[1]), sb_bias)
    y = jnp.concatenate([ret_out.astype(h.dtype), sb.reshape(b, t, W_SB).astype(h.dtype)], -1) @ w_out
    return y, s_new, ks, vs

def causal_dwconv(full, w):
    return lax.conv_general_dilated(full, w[:, None, :].astype(full.dtype), (1,), 'VALID',
                                    dimension_numbers=('NWC', 'WIO', 'NWC'),
                                    feature_group_count=full.shape[-1])

def conformer_conv(h, buf, w1, b1, dw, dwb, ln_g, ln_b, w2, b2):
    a, gt = jnp.split(h @ w1 + b1, 2, axis=-1)
    u = a * jax.nn.sigmoid(gt)
    full = jnp.concatenate([buf.astype(u.dtype), u], axis=1)
    c = layernorm(causal_dwconv(full, dw) + dwb, ln_g, ln_b)
    return jax.nn.silu(c) @ w2 + b2, full[:, -(CONV_W - 1):]

def cross_attn(h, mk, mv, wq, wo):
    b, t, _ = h.shape
    q = (h @ wq).reshape(b, t, H_X, HD_X)
    s = jnp.einsum('bthd,bmhd->bhtm', q, mk.astype(q.dtype)).astype(jnp.float32) * (HD_X ** -0.5)
    p = jax.nn.softmax(s, axis=-1)
    o = jnp.einsum('bhtm,bmhd->bthd', p.astype(h.dtype), mv.astype(h.dtype))
    return o.reshape(b, t, D_MODEL) @ wo

def conv_ffn(h, buf, w_up, dw, dwb, w_down):
    u = h @ w_up
    full = jnp.concatenate([buf.astype(u.dtype), u], axis=1)
    gt, val = jnp.split(causal_dwconv(full, dw) + dwb, 2, axis=-1)
    return (jax.nn.silu(gt) * val) @ w_down, full[:, -(FFN_CONV_W - 1):]

def setup_inputs(seed: int = 0) -> dict:
    key = jax.random.key(seed)
    ks = iter(jax.random.split(key, 40))
    def nrm(shape, scale):
        return jax.random.normal(next(ks), shape, jnp.float32) * scale
    def gain(shape):
        return 1.0 + nrm(shape, 0.05)
    n_pages = PAST_LEN // PAGE_SIZE
    n_used = DEC_BATCH * n_pages
    n_phys = n_used + (n_used + 3) // 4
    page_table = jax.random.permutation(next(ks), n_phys)[:n_used].reshape(DEC_BATCH, n_pages).astype(jnp.int32)
    d = D_MODEL
    return {
        "x_prompt": nrm((BATCH, SEQ, d), 1.0),
        "x_sample": nrm((DEC_BATCH, DEC_SEQ, d), 1.0),
        "cache_sb_k": nrm((N_EVEN, n_phys, PAGE_SIZE, H_SB, HD_SB), 1.0),
        "cache_sb_v": nrm((N_EVEN, n_phys, PAGE_SIZE, H_SB, HD_SB), 1.0),
        "state_ret": nrm((N_EVEN, DEC_BATCH, H_RET, DK_RET, DV_RET), 0.3),
        "state_conv": nrm((N_ODD, DEC_BATCH, CONV_W - 1, d), 0.5),
        "state_ffn_conv": nrm((DEPTH, DEC_BATCH, FFN_CONV_W - 1, 2 * D_FF), 1.0),
        "cache_mem_k": nrm((DEPTH, DEC_BATCH, N_MEM, H_X, HD_X), 1.0),
        "cache_mem_v": nrm((DEPTH, DEC_BATCH, N_MEM, H_X, HD_X), 1.0),
        "page_table": page_table,
        "mem_prompt": nrm((BATCH, N_MEM, d), 1.0),
        "g_mix": gain((DEPTH, d)),
        "w_in_ab": nrm((N_EVEN, d, D_IN_AB), d ** -0.5),
        "ret_gn_g": gain((N_EVEN, W_RV)),
        "w_out_ab": nrm((N_EVEN, D_OUT_AB, d), D_OUT_AB ** -0.5),
        "sb_bias": (-6.0 - jnp.arange(H_SB, dtype=jnp.float32))[None, :] + nrm((N_EVEN, H_SB), 0.1),
        "cv_w1": nrm((N_ODD, d, 2 * d), d ** -0.5),
        "cv_b1": nrm((N_ODD, 2 * d), 0.02),
        "cv_dw": nrm((N_ODD, CONV_W, d), CONV_W ** -0.5),
        "cv_dwb": nrm((N_ODD, d), 0.02),
        "cv_ln_g": gain((N_ODD, d)),
        "cv_ln_b": nrm((N_ODD, d), 0.02),
        "cv_w2": nrm((N_ODD, d, d), d ** -0.5),
        "cv_b2": nrm((N_ODD, d), 0.02),
        "g_cross": gain((DEPTH, d)),
        "xa_wq": nrm((DEPTH, d, d), d ** -0.5),
        "xa_wk": nrm((DEPTH, d, d), d ** -0.5),
        "xa_wv": nrm((DEPTH, d, d), d ** -0.5),
        "xa_wo": nrm((DEPTH, d, d), d ** -0.5),
        "g_ffn": gain((DEPTH, d)),
        "ffn_w_up": nrm((DEPTH, d, 2 * D_FF), d ** -0.5),
        "ffn_dw": nrm((DEPTH, FFN_CONV_W, 2 * D_FF), FFN_CONV_W ** -0.5),
        "ffn_dwb": nrm((DEPTH, 2 * D_FF), 0.02),
        "ffn_w_down": nrm((DEPTH, D_FF, d), D_FF ** -0.5),
        "g_final": gain((d,)),
    }

def reference(x_prompt, x_sample, cache_sb_k, cache_sb_v, state_ret, state_conv, state_ffn_conv,
              cache_mem_k, cache_mem_v, page_table, mem_prompt,
              g_mix, w_in_ab, ret_gn_g, w_out_ab, sb_bias,
              cv_w1, cv_b1, cv_dw, cv_dwb, cv_ln_g, cv_ln_b, cv_w2, cv_b2,
              g_cross, xa_wq, xa_wk, xa_wv, xa_wo,
              g_ffn, ffn_w_up, ffn_dw, ffn_dwb, ffn_w_down, g_final):
    log_gamma = jnp.log1p(-jnp.exp2(-5.0 - jnp.arange(H_RET, dtype=jnp.float32)))
    pos_p = jnp.arange(x_prompt.shape[1])
    pos_s = PAST_LEN + jnp.arange(x_sample.shape[1])
    bp = x_prompt.shape[0]
    xp, xs = x_prompt, x_sample
    sbk_p, sbv_p, sbk_s, sbv_s, ret_p, ret_s = [], [], [], [], [], []
    cv_p, cv_s, ff_p, ff_s, mk_p, mv_p = [], [], [], [], [], []
    for l in range(DEPTH):
        hp = rmsnorm(xp, g_mix[l])
        hs = rmsnorm(xs, g_mix[l])
        if l % 2 == 0:
            e = l // 2
            yp, sp, kp, vp = mixer_ab(hp, pos_p, None, None, None, w_in_ab[e], ret_gn_g[e], w_out_ab[e], sb_bias[e], log_gamma)
            past_k = gather_pages(cache_sb_k[e], page_table)
            past_v = gather_pages(cache_sb_v[e], page_table)
            ys, ss, ksn, vsn = mixer_ab(hs, pos_s, state_ret[e], past_k, past_v, w_in_ab[e], ret_gn_g[e], w_out_ab[e], sb_bias[e], log_gamma)
            sbk_p.append(kp); sbv_p.append(vp); sbk_s.append(ksn); sbv_s.append(vsn)
            ret_p.append(sp); ret_s.append(ss)
        else:
            o = l // 2
            zero_buf = jnp.zeros((bp, CONV_W - 1, D_MODEL), xp.dtype)
            yp, bufp = conformer_conv(hp, zero_buf, cv_w1[o], cv_b1[o], cv_dw[o], cv_dwb[o], cv_ln_g[o], cv_ln_b[o], cv_w2[o], cv_b2[o])
            ys, bufs = conformer_conv(hs, state_conv[o], cv_w1[o], cv_b1[o], cv_dw[o], cv_dwb[o], cv_ln_g[o], cv_ln_b[o], cv_w2[o], cv_b2[o])
            cv_p.append(bufp); cv_s.append(bufs)
        xp = xp + yp
        xs = xs + ys
        mk = (mem_prompt @ xa_wk[l]).reshape(bp, N_MEM, H_X, HD_X)
        mv = (mem_prompt @ xa_wv[l]).reshape(bp, N_MEM, H_X, HD_X)
        mk_p.append(mk); mv_p.append(mv)
        xp = xp + cross_attn(rmsnorm(xp, g_cross[l]), mk, mv, xa_wq[l], xa_wo[l])
        xs = xs + cross_attn(rmsnorm(xs, g_cross[l]), cache_mem_k[l], cache_mem_v[l], xa_wq[l], xa_wo[l])
        zero_ff = jnp.zeros((bp, FFN_CONV_W - 1, 2 * D_FF), xp.dtype)
        fp, fbp = conv_ffn(rmsnorm(xp, g_ffn[l]), zero_ff, ffn_w_up[l], ffn_dw[l], ffn_dwb[l], ffn_w_down[l])
        fs, fbs = conv_ffn(rmsnorm(xs, g_ffn[l]), state_ffn_conv[l], ffn_w_up[l], ffn_dw[l], ffn_dwb[l], ffn_w_down[l])
        ff_p.append(fbp); ff_s.append(fbs)
        xp = xp + fp
        xs = xs + fs
    y_prompt = rmsnorm(xp, g_final)
    y_sample = rmsnorm(xs, g_final)
    sb_k_prompt = jnp.stack(sbk_p); sb_v_prompt = jnp.stack(sbv_p)
    sb_k_sample = jnp.stack(sbk_s); sb_v_sample = jnp.stack(sbv_s)
    ret_prompt = jnp.stack(ret_p); ret_sample = jnp.stack(ret_s)
    conv_prompt = jnp.stack(cv_p); conv_sample = jnp.stack(cv_s)
    ffn_prompt = jnp.stack(ff_p); ffn_sample = jnp.stack(ff_s)
    mem_k_prompt = jnp.stack(mk_p); mem_v_prompt = jnp.stack(mv_p)
    return (y_prompt, y_sample, sb_k_prompt, sb_v_prompt, sb_k_sample, sb_v_sample,
            ret_prompt, ret_sample, conv_prompt, conv_sample, ffn_prompt, ffn_sample,
            mem_k_prompt, mem_v_prompt)


_drawn_inputs = setup_inputs


def setup_inputs(seed=0):
    import zlib

    import numpy as np

    out = dict(_drawn_inputs(seed))
    spreads = {}
    factors = {'cache_sb_k': 2.863,
     'cv_dwb': 3.012,
     'cv_ln_b': 5.605,
     'cv_b2': 3.755,
     'g_cross': 7.835,
     'ffn_dwb': 2.963}
    for name, (base, spread) in spreads.items():
        noise = np.random.default_rng([zlib.crc32(name.encode()), seed]).standard_normal(out[name].shape)
        drawn = base * np.exp(spread * noise) if base else spread * noise
        out[name] = __import__('jax').numpy.asarray(drawn.astype(out[name].dtype))
    for name, factor in factors.items():
        out[name] = (out[name] * factor).astype(out[name].dtype)
    return out
```

```python
from contextlib import ExitStack

import numpy as np

import concourse.bass as bass
from concourse import mybir

F32 = mybir.dt.float32
F32R = mybir.dt.float32r
I32 = mybir.dt.int32
ALU = mybir.AluOpType
ACT = mybir.ActivationFunctionType
AXX = mybir.AxisListType.X

P = 128
D = 1024
KC = D // P
T = 1024
NS = 8
N = T + NS
GRP = 3
GN = N // GRP
TT = T // P
H = 4
PAST = 1024
PG = PAST // P
NPAGES = 80
MEM = 256
MT = MEM // P
HDX = D // H
FF = 2816
FC = FF // P
SEC = FC // 2
W_CONV = 31
EPS = 1e-6
BIG = 1e30
HD = 128
SCALE = float(HD) ** -0.5
SCALE_X = float(HDX) ** -0.5
UW = T + W_CONV - 1

CFP = 3 + W_CONV
PCOL = {}
_at = 0
for _name, _n in (("g_mix", 2 * KC), ("g_cross", 2 * KC), ("g_ffn", 2 * KC), ("g_final", KC),
                  ("gn", H), ("sb_bias", H), ("cf", KC * CFP), ("ln_g", KC), ("ln_b", KC), ("b2", KC),
                  ("ffn0", SEC * 16), ("ffn1", SEC * 16)):
    PCOL[_name] = _at
    _at += _n
NPAR = _at

C_ID, C_TRI, C_ONE, C_LIM, C_EPS = 0, P, 2 * P, 3 * P, 4 * P
HB = 2 * P + 4
C_HEAD = 4 * P + 4
NCON = C_HEAD + H * HB

T_SB, T_RET, T_OUT = 0, 12, 28
T_WQ0, T_FFN0 = 36, 52
T_W1, T_W2 = 118, 134
T_WQ1, T_FFN1 = 142, 158
NT = 224


def build(nc, x_in, mem_in, wts, memw, cons, rope, selc, par, stc, stf0, stf1, stret,
          cache_k, cache_v, cmk, cmv, ptab,
          y, o_sbk, o_sbv, o_retp, o_rets, o_cvp, o_cvs, o_ffn0, o_ffn1, o_st0, o_st1, o_mk, o_mv):
    with ExitStack() as ctx:
        base_at = nc.sbuf_base + (-nc.sbuf_base) % 64
        top = [base_at]

        def place(name, shape, dt=F32, at=None):
            size = 4 * int(np.prod(shape[1:]))
            size += -size % 32
            if at is None:
                at = top[0]
                top[0] += size
            return nc.alloc_sbuf_tensor_at(name, shape, dt, offset=at), at + size

        def keep(name, shape, dt=F32):
            return place(name, shape, dt)[0]

        where = {}

        def layout(items, at):
            out = {}
            for name, shape, *dt in items:
                where[name] = at
                out[name], at = place(name, shape, *(dt or (F32,)), at)
            assert at <= nc.sbuf_usable_end, (items[0][0], at, nc.sbuf_usable_end)
            return out, at

        def sem(name):
            return ctx.enter_context(nc.semaphore(name))

        x_at = top[0]
        X = keep("X", [P, KC, N])
        Hh = keep("Hh", [P, KC, N], F32R)
        Hl = keep("Hl", [P, KC, N], F32R)
        wraw = keep("wraw", [P, 2, 1024])
        Wh = keep("Wh", [P, 2, 1024], F32R)
        Wl = keep("Wl", [P, 2, 1024], F32R)
        con = keep("con", [P, NCON])
        prm = keep("prm", [P, NPAR])
        sel = keep("sel", [NS, NS, P])
        scr = top[0]
        ident = con[:, C_ID:C_ID + P]
        tri = con[:, C_TRI:C_TRI + P]
        ones = con[:, C_ONE:C_ONE + P]
        lim = con[:, C_LIM:C_LIM + P]
        eps = con[:, C_EPS:C_EPS + 1]
        one = con[:, C_ONE:C_ONE + 1]

        nrm, nrm_end = layout([("sq", [P, 2, N]), ("acc", [P, N]), ("rst", [P, N]), ("hf", [P, 2, N])], scr)
        C, _ = place("C", [P, KC, N], F32, x_at)
        mx, mix_at = layout([("qsel", [P, H, NS]), ("qtok", [NS, H * P])], scr)
        sb, _ = layout([("sq_", [P, N]), ("sk_", [P, N]), ("svT", [P, N]), ("svt", [P, TT, P]),
                        ("zs", [P, 3, 512]), ("ab", [P, 512]), ("ex", [P, 512]), ("lg", [P, 2, 512]),
                        ("sp", [P, 2, 512]), ("rr", [P, 2, 512]), ("ea", [P, 2, 512]),
                        ("aa", [P, 2, 512])], mix_at)
        rt, _ = layout([("cs", [P, 2, N]), ("rq", [P, N]), ("rk", [P, N]), ("rvT", [P, N]), ("rg", [P, N]),
                        ("t1", [P, N]), ("t2", [P, N]), ("vt", [P, TT, P]), ("kt", [P, TT, P]),
                        ("st", [P, TT + 1, P]), ("s0", [P, NS, P]),
                        ("hb", [P, HB]), ("kvs", [NS, 2, P]), ("kms", [NS, NS, P]), ("selp", [NS, 2, P]),
                        ("kpg", [P, 2, H * P]), ("vpg", [P, 2, H * P]), ("zz", [P, 9, 64]),
                        ("junk", [P, 2, H * P]), ("pt", [1, NS * PG], I32)], mix_at)
        rt["sm"], rt["qd"] = (rt[x][:, 0:T].rearrange("p (c n) -> p c n", c=TT) for x in ("t1", "t2"))
        cr, cr_at = layout([("qx", [P, KC, N]), ("mkT", [P, KC, MEM]), ("mv", [P, MT, D]),
                            ("qtx", [NS, D])], scr)
        nmem, _ = layout([("memT", [P, KC, MEM]), ("mw", [P, 3, 1024])], cr_at)
        at, _ = layout([("p", [P, 2, 4, MEM]), ("pT", [P, 2, MT, 512]), ("mst", [P, 2, 3, 4])], cr_at)
        c3, _ = layout([("ck", [P, 2, D]), ("cv", [P, 2, D]), ("zc", [P, MT, 32]), ("zst", [32, 4]),
                        ("pr", [32, MEM]), ("pts", [P, MT, 32]), ("junk2", [P, 2, D])], scr)
        cf, cf_at = layout([("cvo", [P, KC, N]), ("uu", [P, 2, UW + NS]), ("sg", [P, N]),
                            ("us", [P, KC, NS, W_CONV]), ("utl", [P, KC, W_CONV - 1]),
                            ("usj", [P, NS, W_CONV]), ("ca", [P, N]), ("cpar", [P, 2, CFP])], scr)
        ln, _ = layout([("lsq", [P, 2, N]), ("lrst", [P, N])], where["uu"])
        ln.update(layout([("lhf", [P, 2, N])], where["usj"])[0])
        ff, _ = layout([("Gh", [P, 2, 2, N], F32R), ("Gl", [P, 2, 2, N], F32R), ("ub", [P, 2, N + 2]),
                        ("cb", [P, 2, N]), ("gf", [P, N]), ("stf", [P, SEC, 64]), ("tls", [P, SEC, 40]),
                        ("fp", [P, 80]), ("ftl", [P, 40])], scr)

        ps = ctx.enter_context(nc.psum_tensor("ps", [P, 8, 512], F32))

        def pset(s, p0=0, p1=P):
            return ps[p0:p1, 3 * s:3 * s + 3, 0:GN]

        def grp(row):
            return row.rearrange("p (g n) -> p g n", g=GRP)

        w_raw = [sem("w_raw0"), sem("w_raw1")]
        w_hi = sem("w_hi")
        w_split = sem("w_split")
        tile_done = sem("tile_done")
        set_free = [sem("set_free0"), sem("set_free1")]
        end_pe, end_dve, end_act = sem("end_pe"), sem("end_dve"), sem("end_act")
        ld_con = sem("ld_con")
        ld_x = [sem(f"ld_x{c}") for c in range(KC // 2)]
        stored = sem("stored")
        kpg_free, vpg_free = sem("kpg_free"), sem("vpg_free")
        made = {}

        def ss(name):
            if name not in made:
                made[name] = sem(name)
            return made[name]

        COUNTS = {
            "ld_mem": 16, "ld_mw_0": 96, "ld_mw_1": 80, "ld_mw_2": 80, "mw_used": 16, "mk_ev": KC, "mv_ev": 2,
            "x_qt": 1, "x_qtc": 2, "x_e": 32, "x_s": 8, "x_p": 8, "x_t": 8, "x_pt0": 8, "x_pt1": 8, "x_o": 16,
            "x_oh": 16, "x_ol": 16, "x_m": 8, "x_r": 8, "ck_used": NS * MT, "cv_used": NS * MT,
            "ld_ck_0": 128, "ld_ck_1": 128, "ld_cv_0": 128, "ld_cv_1": 128, "xs_qb": NS, "xs_t": 2, 
            "xs_soft": 4, "xs_e": 1, "xs_oh": 1, "f_dn": 6 * SEC, "g_lo": FC, "g_hi": FC,
            "f_fp": SEC, "f_gm": FC, "f_c": 16 * SEC, "f_sl": FC, "f_ft": 4 * SEC, "f_tl": SEC, "ld_stf": 16,
        }

        def of_layer(l, name, n):
            return ss(name), n + l * COUNTS[name]

        def ended(e, n):
            for s in (end_pe, end_dve, end_act):
                e.wait_ge(s, n)

        def end_stage(e, mine, n):
            e.drain().then_inc(mine, 1)
            ended(e, n)

        E_SB = 2
        E_RET = E_SB + H
        E_OUT = E_RET + 1
        E_CR0 = E_OUT + 4
        E_FF0 = E_CR0 + 1
        E_CF = E_FF0 + 2
        E_CR1 = E_CF + 4
        E_FF1 = E_CR1 + 1

        F_OUT, F_WQ0, F_FF0 = 0, 4, 12
        F_W1 = F_FF0 + 6 * SEC
        F_W2, F_WQ1, F_FF1 = F_W1 + 8, F_W1 + 12, F_W1 + 20
        CR = ((0, E_OUT, 1, T_WQ0, F_WQ0), (1, E_CF, 4, T_WQ1, F_WQ1))

        UNITS = []
        for half in (1, 0):
            for j in range(4 * half + 3, -1, -1):
                q0 = max(512 * half, P * j)
                UNITS.append((half, j, q0, 512 * (half + 1) - q0))
        NU = len(UNITS)
        DIAG = {u: n for n, u in enumerate(u for u, (half, j, _, _) in enumerate(UNITS) if j >= 4 * half)}
        NDIAG = len(DIAG)
        LATER = {u: n for n, u in enumerate(u for u, (_, j, _, _) in enumerate(UNITS) if j)}
        NLATER = len(LATER)

        block = ctx.enter_context(nc.Block())

        @block.sync
        def _(sp):
            def load(dst, src, s):
                sp.dma_start(dst, src).then_inc(s, 16)

            def weight(t, slot, first=False):
                if not first:
                    sp.wait_ge(w_split, t - 1)
                load(wraw[:, slot:slot + 1, :], wts[bass.ds(t, 1)].rearrange("a p n -> p a n"), w_raw[slot])

            def weights(t0, t1):
                with sp.Fori(0, (t1 - t0) // 2) as i:
                    for j in range(2):
                        weight(2 * i + (t0 + j), j)

            def page(cache, n, i, ring, name, used):
                at_page = sp.value_load(rt["pt"][0:1, bass.ds(16 * i + n, 1)], min_val=0, max_val=NPAGES - 1)
                sp.wait_ge(used, 16 * i + (n + 1))
                load(ring[:, n % 2:n % 2 + 1, :], cache[bass.ds(at_page, 1)].rearrange("a p n -> p a n"),
                     ss(f"{name}{n % 2}"))

            def load_x(c):
                load(X[:, 2 * c:2 * c + 2, :], x_in[:, 2 * c:2 * c + 2, :], ld_x[c])

            load_x(0)
            load(con[:, :], cons, ld_con)
            load(prm[:, :], par, ld_con)
            load(sel[:, :, :], selc, ld_con)
            for j in range(2):
                weight(j, j, first=True)
            for c in range(1, KC // 2):
                load_x(c)
            weights(2, T_RET + 2)
            ended(sp, E_SB)
            load(rt["cs"][:, :, :], rope, ss("ld_rope"))
            load(rt["pt"][:, :], ptab, ss("ld_pt"))
            sp.wait_ge(ss("ld_pt"), 16)
            with sp.Fori(0, H) as i:
                ended(sp, i + E_SB)
                load(rt["s0"][:, :, :], stret[bass.ds(i, 1)].rearrange("h d b e -> d (h b) e"), ss("ld_s0"))
                for j in range(4):
                    weight(4 * i + (T_RET + 2 + j), j % 2)
                for n in range(16):
                    page(cache_k, n, i, rt["kpg"], "ld_k", kpg_free)
                for n in range(16):
                    page(cache_v, n, i, rt["vpg"], "ld_v", vpg_free)
            for c in range(KC // 2):
                sp.wait_ge(ss("c_lo"), 2 * c + 2)
                load_x(c)
            weights(T_OUT + 2, T_WQ0 + 2)

            def cross(l, e0, t0):
                ended(sp, e0)
                load(nmem["memT"][:, :, :], mem_in, ss("ld_mem"))
                for t in range(16):
                    if t >= 3:
                        sp.wait_ge(*of_layer(l, "mw_used", t - 2))
                    load(nmem["mw"][:, t % 3, :], memw[16 * l + t], ss(f"ld_mw_{t % 3}"))
                weights(t0 + 2, t0 + 10)
                ended(sp, e0 + 2)
                for what, cache in (("ck", cmk), ("cv", cmv)):
                    for n in range(NS * MT):
                        if n >= 2:
                            sp.wait_ge(*of_layer(l, f"{what}_used", n - 1))
                        load(c3[what][:, n % 2, :], cache[l, n // MT, n % MT * P:(n % MT + 1) * P],
                             ss(f"ld_{what}_{n % 2}"))
                weights(t0 + 10, t0 + 18)

            def ffn(l, e0, t0, t1):
                ended(sp, e0)
                load(ff["stf"][:, :, :], (stf0, stf1)[l], ss("ld_stf"))
                weights(t0 + 2, t1)

            cross(0, E_OUT, T_WQ0)
            ffn(0, E_CR0, T_FFN0, T_W1 + 2)
            ended(sp, E_FF0)
            load(cf["us"][:, :, :, 0:W_CONV - 1], stc, ss("ld_us"))
            weights(T_W1 + 2, T_WQ1 + 2)
            cross(1, E_CF, T_WQ1)
            ffn(1, E_CR1, T_FFN1, NT)

        @block.gpsimd
        def _(pool):
            for s in set_free:
                pool.sem_inc(s, 1)
            for s in (kpg_free, vpg_free):
                pool.sem_inc(s, 2)

            def split(t, j, landed, first=False):
                pool.wait_ge(w_raw[j], landed)
                if not first:
                    pool.wait_ge(tile_done, t - 1)
                pool.tensor_tensor(Wh[:, j, :], wraw[:, j, :], one.broadcast_to((P, 1024)),
                                   ALU.mult).then_inc(w_hi, 1)
                pool.wait_ge(w_hi, t + 1)
                pool.tensor_tensor(Wl[:, j, :], wraw[:, j, :], Wh[:, j, :].bitcast(F32),
                                   ALU.subtract).then_inc(w_split, 1)

            pool.wait_ge(ld_con, 48)
            for j in range(2):
                split(j, j, 16, first=True)
            with pool.Fori(1, NT // 2) as i:
                for j in range(2):
                    split(2 * i + j, j, 16 * i + 16)

        @block.tensor
        def _(pe):
            mm = pe.matmul

            def three(outs, wcol, xs, first, last):
                for a, (w, x) in enumerate(((Wh, 0), (Wh, 1), (Wl, 0))):
                    for o, r in zip(outs, xs[x]):
                        ins = mm(o, w[:, wcol[0], wcol[1]:wcol[1] + P], r,
                                 start=first and a == 0, stop=last and a == 2)
                return ins

            def groups(t, k):
                return [t[:, k, g * GN:(g + 1) * GN] for g in range(GRP)]

            def tile(t, slot, s, ready=None):
                pe.wait_ge(w_split, t + 1)
                for k in range(KC):
                    if ready is not None:
                        ready(k)
                    ins = three([ps[:, 3 * s + g, 0:GN] for g in range(GRP)], (slot, k * P),
                                (groups(Hh, k), groups(Hl, k)), k == 0, k == KC - 1)
                ins.then_inc(tile_done, 1)

            def product(t0, npairs, freed, ready):
                def pair(i, first):
                    for s in range(2):
                        pe.wait_ge(set_free[s], i + (freed + 1))
                        tile(2 * i + (t0 + s), s, s, ready if first and s == 0 else None)

                pair(0, True)
                with pe.Fori(1, npairs) as i:
                    pair(i, False)

            def column_sums(src, s, done):
                for g in range(GRP):
                    ins = mm(ps[:, 3 * s + g, 0:GN], ones, src[:, g * GN:(g + 1) * GN], start=True, stop=True)
                ins.then_inc(done, 1)

            def norm_sum(nk):
                pe.wait_ge(ss("n_acc"), KC * (nk + 1))
                column_sums(nrm["acc"], 0, ss("n_sum"))

            def split_ready(nk):
                return lambda k: pe.wait_ge(ss("n_lo"), KC * nk + k + 1)

            pe.wait_ge(ld_con, 48)
            norm_sum(0)
            with pe.Fori(0, 2) as i:
                for hh in range(2):
                    h = 2 * i + hh
                    if hh:
                        pe.wait_ge(ss("sb_ea"), NU * h)
                    for j in range(3 * hh, 3 * hh + 3):
                        if j % 3 == 2:
                            pe.wait_ge(ss("sb_q"), h + 1)
                        tile(6 * i + (T_SB + j), j % 2, j % 2, split_ready(0))
                    pe.wait_ge(ss("sb_v"), h + 1)
                    if hh:
                        pe.wait_ge(ss("sb_oev"), 2 * h)
                    for c in range(TT):
                        ins = pe.transpose(ps[:, 6 + c // 4, (c % 4) * P:(c % 4 + 1) * P],
                                           sb["svT"][:, c * P:(c + 1) * P], ident)
                    ins.then_inc(ss("sb_vt"), 1)
                    pe.wait_ge(ss("sb_q"), h + 1)
                    pe.wait_ge(ss("sb_k"), h + 1)

                    def scores(u):
                        half, j, q0, w = UNITS[u]
                        if u >= 2 or hh:
                            pe.wait_ge(ss("sb_zs"), NU * h + (u - 1))
                        mm(ps[:, u % 2, 0:w], sb["sk_"][:, j * P:(j + 1) * P], sb["sq_"][:, q0:q0 + w],
                           start=True, stop=True).then_inc(ss("sb_z"), 1)

                    def sums(u):
                        half, j, q0, w = UNITS[u]
                        lone = j == 4 * half + 3
                        pe.wait_ge(ss("sb_sp"), NU * h + (u + 1))
                        if u >= 2 or hh:
                            pe.wait_ge(ss("sb_ea"), NU * h + (u - 1))
                        ins = mm(ps[:, 2 + u % 2, 0:w], tri, sb["sp"][:, u % 2, 0:w], start=True, stop=lone)
                        if not lone:
                            pe.wait_ge(ss("sb_rr"), NLATER * h + LATER[u - 1] + 1)
                            ins = mm(ps[:, 2 + u % 2, 0:w], ones, sb["rr"][:, u % 2, q0 - 512 * half:512],
                                     start=False, stop=True)
                        ins.then_inc(ss("sb_s"), 1)

                    def values(u):
                        half, j, q0, w = UNITS[u]
                        if u == 0:
                            pe.wait_ge(ss("sb_vev"), 2 * h + 2)
                        pe.wait_ge(ss("sb_aa"), NU * h + (u + 1))
                        mm(ps[:, 6 + half, q0 - 512 * half:512], sb["svt"][:, j, :], sb["aa"][:, u % 2, 0:w],
                           start=j == 4 * half + 3, stop=j == 0, skip_group_check=True).then_inc(ss("sb_o"), 1)

                    scores(0)
                    for u in range(NU):
                        if u + 1 < NU:
                            scores(u + 1)
                        sums(u)
                        if u:
                            values(u - 1)
                    values(NU - 1)
                end_stage(pe, end_pe, i + 1)

            for h in range(H):
                ins = pe.transpose(ps[0:NS, 6, h * P:(h + 1) * P], mx["qsel"][:, h, :], ident)
            ins.then_inc(ss("r_qt"), 1)
            with pe.Fori(0, H) as i:
                for j in range(4):
                    if j >= 2:
                        pe.wait_ge(ss("r_qp" if j == 2 else "r_kp"), i + 1)
                    tile(4 * i + (T_RET + j), j % 2, j % 2)
                pe.wait_ge(ss("r_qtc"), 1)
                pe.wait_ge(ss("r_v"), i + 1)
                for c in range(TT):
                    ins = pe.transpose(ps[:, 6 + c // 4, (c % 4) * P:(c % 4 + 1) * P],
                                       rt["rvT"][:, c * P:(c + 1) * P], ident)
                ins.then_inc(ss("r_vT"), 1)
                pe.wait_ge(ss("r_q"), i + 1)
                pe.wait_ge(ss("r_k"), i + 1)
                pe.wait_ge(ss("r_g"), i + 1)
                for c in range(TT):
                    pe.transpose(ps[:, c // 4, (c % 4) * P:(c % 4 + 1) * P],
                                 rt["rk"][:, c * P:(c + 1) * P], ident)
                pe.transpose(ps[0:NS, 2, 0:P], rt["rk"][:, T:N], ident)
                pe.transpose(ps[0:NS, 2, P:2 * P], rt["rvT"][:, T:N], ident).then_inc(ss("r_kT"), 1)
                for c in range(TT):
                    ins = mm(ps[:, 3 + c // 4, (c % 4) * P:(c % 4 + 1) * P], rt["rk"][:, c * P:(c + 1) * P],
                             rt["rq"][:, c * P:(c + 1) * P], start=True, stop=True)
                ins.then_inc(ss("r_sc"), 1)
                pe.wait_ge(ss("r_kt"), 2 * i + 2)
                pe.wait_ge(ss("r_vt"), 2 * i + 2)
                for c in range(TT):
                    ins = mm(ps[:, c // 4, (c % 4) * P:(c % 4 + 1) * P], rt["kt"][:, c, :], rt["vt"][:, c, :],
                             start=True, stop=True)
                ins.then_inc(ss("r_up"), 1)
                pe.wait_ge(ss("r_sm"), 2 * i + 2)
                pe.wait_ge(ss("r_kms"), i + 1)
                for b in range(NS):
                    ins = mm(ps[:, 3 + b // 4, (b % 4) * P:(b % 4 + 1) * P], rt["kms"][:, b, :],
                             rt["kvs"][:, 1, :], start=True, stop=True)
                ins.then_inc(ss("r_sup"), 1)
                pe.wait_ge(ss("r_st"), TT * i + TT)
                pe.wait_ge(ss("r_qd"), i + 1)
                for c in range(TT):
                    o = ps[:, 6 + c // 4, (c % 4) * P:(c % 4 + 1) * P]
                    mm(o, rt["vt"][:, c, :], rt["sm"][:, c, :], start=True, stop=False)
                    mm(o, rt["st"][:, c, :], rt["qd"][:, c, :], start=False, stop=True)
                pe.wait_ge(ss("r_s1"), 2 * i + 2)
                for b in range(NS):
                    ins = mm(ps[:, 2, 256 + b:257 + b], rt["s0"][:, b, :], rt["rq"][:, T + b:T + b + 1],
                             start=True, stop=True)
                ins.then_inc(ss("r_o"), 1)
                pe.wait_ge(ss("r_of"), 2 * i + 2)
                column_sums(rt["t1"], 0, ss("r_mu"))
                pe.wait_ge(ss("r_dsq"), i + 1)
                column_sums(rt["t1"], 1, ss("r_var"))
                for b in range(2):
                    pe.wait_ge(ss("r_selp"), i + 1)
                    if b:
                        pe.wait_ge(kpg_free, 16 * i + (2 + PG))
                    mm(ps[:, 6, :], rt["selp"][:, b, :], mx["qtok"][:, :], start=True, stop=True)\
                        .then_inc(ss("r_qb"), 1)
                pe.wait_ge(ss("y_sp"), i + 1)
                pe.wait_ge(ss("y_rr"), i + 1)
                mm(ps[:, 5, 0:64], tri, rt["zz"][:, 5, :], start=True, stop=False)
                mm(ps[:, 5, 0:64], ones, rt["zz"][:, 6, :], start=False, stop=True).then_inc(ss("y_s"), 1)
                pe.wait_ge(ss("y_a"), i + 1)
                for n in range(16):
                    b, g = n // PG, n % PG
                    pe.wait_ge(ss(f"ld_v{n % 2}"), 128 * i + 16 * (n // 2 + 1))
                    for h in range(H):
                        col = g * 8 + b * 4 + h
                        ins = mm(ps[:, 7, 4 * b + h:4 * b + h + 1], rt["vpg"][:, n % 2, h * P:(h + 1) * P],
                                 rt["zz"][:, 8, col:col + 1], start=(n == 0 and h == 0),
                                 stop=(n == 15 and h == H - 1), skip_group_check=True)
                    ins.then_inc(vpg_free, 1)
                end_stage(pe, end_pe, i + (E_SB + 1))

            product(T_OUT, 4, F_OUT, lambda k: pe.wait_ge(ss("c_lo"), k + 1))
            end_stage(pe, end_pe, E_OUT)

            def cross(l, e0, nk, t0, freed):
                pe.wait_ge(*of_layer(l, "ld_mem", 16))
                for c in range(KC):
                    if c == 3:
                        norm_sum(nk)
                    pe.wait_ge(*of_layer(l, f"ld_mw_{c % 3}", 16 * (c // 3 + 1)))
                    if c >= 3:
                        pe.wait_ge(*of_layer(l, "mk_ev", c - 2))
                    for k in range(KC):
                        ins = mm(ps[:, 3 + c % 3, 0:MEM], nmem["mw"][:, c % 3, k * P:(k + 1) * P],
                                 nmem["memT"][:, k, :], start=k == 0, stop=k == KC - 1)
                    ins.then_inc(ss("mw_used"), 1)
                for t in range(8, 16):
                    half, kk = (t - 8) // 4, (t - 8) % 4
                    pe.wait_ge(*of_layer(l, f"ld_mw_{t % 3}", 16 * (t // 3 + 1)))
                    if half and kk == 0:
                        pe.wait_ge(*of_layer(l, "mv_ev", 1))
                    for k in range(2):
                        for m in range(MT):
                            ins = mm(ps[:, 6 + m, :], nmem["memT"][:, 2 * kk + k, m * P:(m + 1) * P],
                                     nmem["mw"][:, t % 3, k * 512:(k + 1) * 512],
                                     start=(kk == 0 and k == 0), stop=(kk == 3 and k == 1))
                    ins.then_inc(ss("mw_used"), 1)
                product(t0, 4, freed, split_ready(nk))
                end_stage(pe, end_pe, e0 + 1)
                for c in range(KC):
                    ins = pe.transpose(ps[0:NS, 6 + c // 4, (c % 4) * P:(c % 4 + 1) * P],
                                       cr["qx"][:, c, T:N], ident)
                ins.then_inc(ss("x_qt"), 1)

                def scores(u):
                    hx, half = u // 2, u % 2
                    if u >= 2:
                        pe.wait_ge(*of_layer(l, "x_e", 4 * (u - 1)))
                    for tt in range(4):
                        for dc in range(2):
                            ins = mm(ps[:, (u % 2) * 2 + tt // 2, (tt % 2) * MEM:(tt % 2 + 1) * MEM],
                                     cr["qx"][:, 2 * hx + dc, (4 * half + tt) * P:(4 * half + tt + 1) * P],
                                     cr["mkT"][:, 2 * hx + dc, :], start=dc == 0, stop=dc == 1)
                    ins.then_inc(ss("x_s"), 1)

                def turn(u):
                    pe.wait_ge(*of_layer(l, "x_p", u + 1))
                    if u:
                        pe.wait_ge(*of_layer(l, "x_pt0", u))
                        pe.wait_ge(*of_layer(l, "x_pt1", u))
                    for m in range(MT):
                        for tt in range(4):
                            ins = pe.transpose(ps[:, 4 + m, tt * P:(tt + 1) * P],
                                               at["p"][:, u % 2, tt, m * P:(m + 1) * P], ident)
                    ins.then_inc(ss("x_t"), 1)

                def weigh(u):
                    hx = u // 2
                    pe.wait_ge(*of_layer(l, "x_pt0", u + 1))
                    pe.wait_ge(*of_layer(l, "x_pt1", u + 1))
                    if u == 0:
                        pe.wait_ge(*of_layer(l, "x_qtc", 2))
                    else:
                        pe.wait_ge(*of_layer(l, "x_ol", 2 * u))
                    for dc in range(2):
                        for m in range(MT):
                            ins = mm(ps[:, 6 + dc, :], cr["mv"][:, m, (2 * hx + dc) * P:(2 * hx + dc + 1) * P],
                                     at["pT"][:, u % 2, m, :], start=m == 0, stop=m == MT - 1)
                        ins.then_inc(ss("x_o"), 1)

                scores(0)
                for u in range(8):
                    if u + 1 < 8:
                        scores(u + 1)
                    turn(u)
                    if u:
                        weigh(u - 1)
                weigh(7)
                end_stage(pe, end_pe, e0 + 2)
                for b in range(NS):
                    if b >= 2:
                        pe.wait_ge(*of_layer(l, "ck_used", MT * (b - 1)))
                    for j in range(2):
                        ins = mm(ps[:, 2 * (b % 2) + j, :], sel[:, b, :], cr["qtx"][:, j * 512:(j + 1) * 512],
                                 start=True, stop=True)
                    ins.then_inc(ss("xs_qb"), 1)
                pe.wait_ge(*of_layer(l, "ck_used", NS * MT))
                for m in range(MT):
                    ins = pe.transpose(ps[0:32, 4, m * P:(m + 1) * P], c3["zc"][:, m, :], ident)
                ins.then_inc(ss("xs_t"), 1)
                pe.wait_ge(*of_layer(l, "xs_soft", 3))
                for m in range(MT):
                    ins = pe.transpose(ps[:, 5, m * 32:(m + 1) * 32], c3["pr"][:, m * P:(m + 1) * P],
                                       con[0:32, C_ID:C_ID + 32])
                ins.then_inc(ss("xs_t"), 1)
                pe.wait_ge(*of_layer(l, "xs_soft", 4))
                for n in range(NS * MT):
                    b, m = n // MT, n % MT
                    pe.wait_ge(*of_layer(l, f"ld_cv_{n % 2}", 16 * (n // 2 + 1)))
                    for c in range(KC):
                        ins = mm(ps[:, 6, c * NS + b:c * NS + b + 1], c3["cv"][:, n % 2, c * P:(c + 1) * P],
                                 c3["pts"][:, m, 4 * b + c // 2:4 * b + c // 2 + 1], start=(n == 0 and c == 0),
                                 stop=(n == NS * MT - 1 and c == KC - 1), skip_group_check=True)
                    ins.then_inc(ss("cv_used"), 1)
                end_stage(pe, end_pe, e0 + 3)
                product(t0 + 8, 4, freed + 4, lambda k: None)
                end_stage(pe, end_pe, e0 + 4)

            def ffn(l, e1, nk, t0, freed):
                norm_sum(nk)

                def up(i, t, f, ready=None):
                    for q in range(4):
                        pe.wait_ge(set_free[q % 2], f + (q // 2 + 1))
                        tile(t + q, q % 2, q % 2, ready if q == 0 else None)

                def down(i, par, t, f):
                    pe.wait_ge(*of_layer(l, "g_lo", 2 * i + 2))
                    for n in range(8):
                        if n % 4 == 0:
                            pe.wait_ge(w_split, t + (n // 4 + 1))
                        pe.wait_ge(set_free[n % 2], f + (n // 2 + 1))
                        for kk in range(2):
                            ins = three([ps[:, 3 * (n % 2) + g, 0:GN] for g in range(GRP)],
                                        (n // 4, kk * 512 + (n % 4) * P),
                                        [[G[:, par, kk, g * GN:(g + 1) * GN] for g in range(GRP)]
                                         for G in (ff["Gh"], ff["Gl"])], kk == 0, kk == 1)
                        ins.then_inc(tile_done if n % 4 == 3 else ss("f_dn"), 1)

                up(0, t0, freed, split_ready(nk))
                with pe.Fori(0, SEC // 2) as r:
                    for j in (1, 2):
                        up(2 * r + j, 12 * r + (t0 + 4 + 6 * (j - 1)), 12 * r + (freed + 2 + 6 * (j - 1)))
                        down(2 * r + (j - 1), (j - 1) % 2, 12 * r + (t0 + 8 + 6 * (j - 1)),
                             12 * r + (freed + 4 + 6 * (j - 1)))
                down(SEC - 1, 0, t0 + 6 * SEC - 2, freed + 6 * SEC - 4)
                end_stage(pe, end_pe, e1)

            cross(*CR[0])
            ffn(0, E_FF0, 2, T_FFN0, F_FF0)
            norm_sum(3)
            product(T_W1, 8, F_W1, split_ready(3))
            end_stage(pe, end_pe, E_FF0 + 1)
            for c in range(KC):
                for g in range(GRP):
                    ins = mm(ps[:, g, 0:GN], ones, cf["cvo"][:, c, g * GN:(g + 1) * GN],
                             start=c == 0, stop=c == KC - 1)
            ins.then_inc(ss("l_mu"), 1)
            for c in range(KC):
                pe.wait_ge(ss("l_sq"), c + 1)
                for g in range(GRP):
                    ins = mm(ps[:, 3 + g, 0:GN], ones, ln["lsq"][:, c % 2, g * GN:(g + 1) * GN],
                             start=c == 0, stop=c == KC - 1)
                ins.then_inc(ss("l_sqs"), 1)
            product(T_W2, 4, F_W2, lambda k: pe.wait_ge(ss("l_lo"), k + 1))
            end_stage(pe, end_pe, E_CF)
            cross(*CR[1])
            ffn(1, E_FF1, 5, T_FFN1, F_FF1)
            norm_sum(6)

        @block.scalar
        def _(act):
            nstored = [0]

            def store(dst, src, times=1):
                act.dma_start(dst, src).then_inc(stored, 16)
                nstored[0] += times

            def fn(out, in_, f, s, **kw):
                ins = act.activation(out, in_, f, **kw)
                if s is not None:
                    ins.then_inc(s, 1)

            def fixed():
                act.wait_ge(ld_con, 48)

            def norm(nk, hi=True, before=lambda c: None):
                for c in range(KC):
                    if nk == 0:
                        act.wait_ge(ld_x[c // 2], 16)
                    if c >= 2:
                        act.wait_ge(ss("n_acc"), KC * nk + c - 1)
                    fn(nrm["sq"][:, c % 2, :], X[:, c, :], ACT.Square, ss("n_sq"))
                act.wait_ge(ss("n_sum"), nk + 1)
                fn(grp(nrm["rst"][:, :]), pset(0), ACT.Sqrt, ss("n_rt"), scale=1.0 / D, bias=eps)
                if hi:
                    for c in range(KC):
                        act.wait_ge(ss("n_hf"), KC * nk + c + 1)
                        fn(Hh[:, c, :], nrm["hf"][:, c % 2, :], ACT.Copy, ss("n_hi"))

            act.wait_ge(ld_con, 48)
            norm(0)
            with act.Fori(0, 2) as i:
                for hh in range(2):
                    h = 2 * i + hh
                    act.wait_ge(tile_done, 6 * i + (T_SB + 3 * hh + 1))
                    fn(grp(sb["sq_"][:, :]), pset(hh), ACT.Copy, ss("sb_q"))
                    act.wait_ge(tile_done, 6 * i + (T_SB + 3 * hh + 3))
                    fn(grp(sb["svT"][:, :]), pset(hh), ACT.Copy, ss("sb_v"))
                    act.wait_ge(ss("sb_k"), h + 1)
                    store(o_sbk[bass.ds(h, 1)].rearrange("h p n -> p (h n)"), sb["sk_"][:, :], 2)
                    act.wait_ge(ss("sb_v"), h + 1)
                    store(o_sbv[bass.ds(h, 1)].rearrange("h p n -> p (h n)"), sb["svT"][:, :], 2)

                    def softplus(u):
                        w = UNITS[u][3]
                        act.wait_ge(ss("sb_zs"), NU * h + (u + 1))
                        fn(sb["ab"][:, 0:w], sb["zs"][:, u % 3, 0:w], ACT.Abs, ss("sb_sp1"))
                        act.wait_ge(ss("sb_sp1"), 2 * NU * h + (2 * u + 1))
                        fn(sb["ex"][:, 0:w], sb["ab"][:, 0:w], ACT.Exp, ss("sb_sp1"), scale=-1.0)
                        act.wait_ge(ss("sb_sp1"), 2 * NU * h + (2 * u + 2))
                        if u >= 2 or hh:
                            act.wait_ge(ss("sb_sp"), NU * h + (u - 1))
                        fn(sb["lg"][:, u % 2, 0:w], sb["ex"][:, 0:w], ACT.Ln, ss("sb_lg"), bias=one)

                    def probs(u):
                        w = UNITS[u][3]
                        act.wait_ge(ss("sb_ea"), NU * h + (u + 1))
                        if u >= 2 or hh:
                            act.wait_ge(ss("sb_o"), NU * h + (u - 1))
                        fn(sb["aa"][:, u % 2, 0:w], sb["ea"][:, u % 2, 0:w], ACT.Exp, ss("sb_aa"))

                    for u in range(NU):
                        softplus(u)
                        if u:
                            probs(u - 1)
                    act.wait_ge(stored, 64 * i + 32 * (hh + 1))
                    probs(NU - 1)
                end_stage(act, end_act, i + 1)
            act.wait_ge(ss("r_qt"), 1)
            fn(mx["qtok"][:, :], ps[0:NS, 6, :], ACT.Copy, ss("r_qtc"))
            with act.Fori(0, H) as i:
                act.wait_ge(tile_done, 4 * i + (T_RET + 3))
                fn(grp(rt["rvT"][:, :]), pset(0), ACT.Copy, ss("r_v"))
                act.wait_ge(tile_done, 4 * i + (T_RET + 4))
                fn(grp(rt["rg"][:, :]), pset(1), ACT.Silu, ss("r_g"))
                act.wait_ge(ss("r_vT"), i + 1)
                for j in range(2):
                    fn(rt["vt"][:, 4 * j:4 * j + 4, :], ps[:, 6 + j, :].rearrange("p (c n) -> p c n", c=4),
                       ACT.Copy, ss("r_vt"))
                act.wait_ge(ss("r_o"), i + 1)
                fn(rt["t1"][:, 0:T].rearrange("p (j n) -> p j n", j=2), ps[:, 6:8, :], ACT.Copy, ss("r_of"))
                fn(rt["t1"][:, T:N], ps[:, 2, 256:256 + NS], ACT.Copy, ss("r_of"))
                act.wait_ge(ss("r_d"), i + 1)
                fn(rt["t1"][:, :], rt["t2"][:, :], ACT.Square, ss("r_dsq"))
                act.wait_ge(ss("r_var"), i + 1)
                fn(grp(rt["rvT"][:, :]), pset(1), ACT.Sqrt, ss("r_rt"), scale=1.0 / P, bias=eps)
                act.wait_ge(ss("r_st"), TT * i + TT)
                store(o_retp[bass.ds(i, 1)].rearrange("h d e -> d (h e)"), rt["st"][:, TT, :], H)
                act.wait_ge(ss("r_s1"), 2 * i + 2)
                store(o_rets[:, bass.ds(i, 1)].rearrange("b h d e -> d (b h) e"), rt["s0"][:, :, :], H)
                z = rt["zz"]
                act.wait_ge(ss("y_z"), i + 1)
                fn(z[:, 2, :], z[:, 1, :], ACT.Abs, ss("y_sp1"))
                act.wait_ge(ss("y_sp1"), 2 * i + 1)
                fn(z[:, 3, :], z[:, 2, :], ACT.Exp, ss("y_sp1"), scale=-1.0)
                act.wait_ge(ss("y_sp1"), 2 * i + 2)
                fn(z[:, 4, :], z[:, 3, :], ACT.Ln, ss("y_lg"), bias=one)
                act.wait_ge(ss("y_ea"), i + 1)
                act.wait_ge(stored, 32 * i + (16 * 8 + 32))
                fn(z[:, 8, :], z[:, 7, :], ACT.Exp, ss("y_a"))
                end_stage(act, end_act, i + (E_SB + 1))
            for c in range(KC):
                fn(Hh[:, c, :], C[:, c, :], ACT.Copy, ss("c_hi"))
            end_stage(act, end_act, E_OUT)

            def cross(l, e0, nk, t0, freed):
                norm(nk)
                for half in range(2):
                    act.wait_ge(*of_layer(l, "mw_used", 8 + 4 * (half + 1)))
                    fn(cr["mv"][:, :, half * 512:(half + 1) * 512], ps[:, 6:8, :], ACT.Copy, ss("mv_ev"))
                act.wait_ge(*of_layer(l, "mk_ev", KC))
                store(o_mk[l], cr["mkT"][:, :, :])
                act.wait_ge(*of_layer(l, "mv_ev", 2))
                store(o_mv[l], cr["mv"][:, :, :])
                end_stage(act, end_act, e0 + 1)
                act.wait_ge(*of_layer(l, "x_qt", 1))
                for j in range(2):
                    fn(cr["qtx"][:, j * 512:(j + 1) * 512], ps[0:NS, 6 + j, :], ACT.Copy, ss("x_qtc"))

                def exps(u):
                    act.wait_ge(*of_layer(l, "x_m", u + 1))
                    if u >= 2:
                        act.wait_ge(*of_layer(l, "x_t", u - 1))
                    for tt in range(4):
                        fn(at["p"][:, u % 2, tt, :],
                           ps[:, (u % 2) * 2 + tt // 2, (tt % 2) * MEM:(tt % 2 + 1) * MEM], ACT.Exp,
                           ss("x_e"), bias=at["mst"][:, u % 2, 0, tt:tt + 1],
                           accum_out=at["mst"][:, u % 2, 1, tt:tt + 1])

                def turned(u):
                    act.wait_ge(*of_layer(l, "x_t", u + 1))
                    if u >= 2:
                        act.wait_ge(*of_layer(l, "x_o", 2 * (u - 1)))
                    fn(at["pT"][:, u % 2, 0, :], ps[:, 4, :], ACT.Copy, ss("x_pt0"))

                def out(u):
                    hx, half = u // 2, u % 2
                    for dc in range(2):
                        act.wait_ge(*of_layer(l, "x_o", 2 * u + dc + 1))
                        fn(Hh[:, 2 * hx + dc, 512 * half:512 * half + 512], ps[:, 6 + dc, :], ACT.Copy,
                           ss("x_oh"))

                exps(0)
                for u in range(8):
                    if u + 1 < 8:
                        exps(u + 1)
                    turned(u)
                    if u:
                        out(u - 1)
                out(7)
                end_stage(act, end_act, e0 + 2)
                act.wait_ge(*of_layer(l, "xs_soft", 1))
                fn(c3["pr"][:, :], ps[0:32, 4, 0:MEM], ACT.Exp, ss("xs_e"), bias=c3["zst"][:, 0:1],
                   accum_out=c3["zst"][:, 1:2])
                act.wait_ge(*of_layer(l, "cv_used", NS * MT))
                fn(Hh[:, :, T:N], ps[:, 6, 0:KC * NS].rearrange("p (c b) -> p c b", c=KC), ACT.Copy,
                   ss("xs_oh"))
                act.wait_ge(stored, 16 * nstored[0])
                end_stage(act, end_act, e0 + 3)
                end_stage(act, end_act, e0 + 4)

            def ffn(l, e1, nk, t0):
                norm(nk)

                def pair(i, k, par, t, first):
                    for v in range(2):
                        q = 2 * k + v
                        if v == 0:
                            act.wait_ge(*of_layer(l, "f_fp", i + 1))
                            if not first:
                                act.wait_ge(*of_layer(l, "f_gm", 2 * i + k))
                        act.wait_ge(tile_done, t + (v + 1))
                        fn(grp(ff["ub"][:, v, 2:N + 2]), pset(v), ACT.Copy, None)
                        fn(grp(ff["cb"][:, v, :]), pset(v), ACT.Identity, set_free[v],
                           scale=ff["fp"][:, 4 * q + 2:4 * q + 3], bias=ff["fp"][:, 4 * q + 3:4 * q + 4])
                        if v == 0:
                            act.wait_ge(*of_layer(l, "f_c", 16 * i + (4 * q + 4)))
                            fn(ff["cb"][:, 0, :], ff["cb"][:, 0, :], ACT.Silu, ss("f_sl"))
                    act.wait_ge(*of_layer(l, "f_gm", 2 * i + (k + 1)))
                    if not isinstance(i, int):
                        act.wait_ge(tile_done, 6 * i + (t0 - 2))
                    fn(ff["Gh"][:, par, k, :], ff["gf"][:, :], ACT.Copy, ss("g_hi"))

                pair(0, 0, 0, t0, True)
                pair(0, 1, 0, t0 + 2, False)
                with act.Fori(0, SEC // 2) as r:
                    for j in (1, 2):
                        for k in range(2):
                            pair(2 * r + j, k, j % 2, 12 * r + (t0 + 4 + 6 * (j - 1) + 2 * k), False)
                act.wait_ge(*of_layer(l, "f_tl", SEC))
                store((o_ffn0, o_ffn1)[l], ff["tls"][:, :, :])
                store((o_st0, o_st1)[l], ff["stf"][:, :, :])
                act.wait_ge(stored, 16 * nstored[0])
                end_stage(act, end_act, e1)

            cross(*CR[0])
            ffn(0, E_FF0, 2, T_FFN0)
            norm(3)
            with act.Fori(0, 4) as i:
                for j in range(2):
                    act.wait_ge(ss("c_par"), i + 1)
                    act.wait_ge(tile_done, 4 * i + (T_W1 + 2 * j + 2))
                    if j:
                        act.wait_ge(ss("c_u"), 2 * i + 1)
                    fn(grp(cf["sg"][:, :]), pset(1), ACT.Sigmoid, set_free[1], bias=cf["cpar"][:, j, 1:2])
                act.wait_ge(ss("c_u"), 2 * i + 2)
            end_stage(act, end_act, E_FF0 + 1)
            store(o_cvp, cf["utl"][:, :, :])
            store(o_cvs, cf["us"][:, :, :, :])
            for c in range(KC):
                act.wait_ge(ss("l_d"), c + 1)
                if c >= 2:
                    act.wait_ge(ss("l_sqs"), c - 1)
                fn(ln["lsq"][:, c % 2, :], cf["cvo"][:, c, :], ACT.Square, ss("l_sq"))
            act.wait_ge(ss("l_sqs"), KC)
            fn(grp(ln["lrst"][:, :]), pset(1), ACT.Sqrt, ss("l_rt"), scale=1.0 / D, bias=eps)
            for c in range(KC):
                act.wait_ge(ss("l_hf"), c + 1)
                fn(ln["lhf"][:, c % 2, :], ln["lhf"][:, c % 2, :], ACT.Silu, ss("l_si"),
                   bias=prm[:, PCOL["ln_b"] + c:PCOL["ln_b"] + c + 1])
                act.wait_ge(ss("l_si"), c + 1)
                fn(Hh[:, c, :], ln["lhf"][:, c % 2, :], ACT.Copy, ss("l_hi"))
            act.wait_ge(stored, 16 * nstored[0])
            end_stage(act, end_act, E_CF)
            cross(*CR[1])
            ffn(1, E_FF1, 5, T_FFN1)
            norm(6, hi=False)
            for c in range(KC):
                act.wait_ge(ss("n_hf"), KC * 6 + c + 1)
                store(y[:, c, :], X[:, c, :])
            act.wait_ge(stored, 16 * nstored[0])

        @block.vector
        def _(dve):
            def tt_(out, a, b, op, s):
                ins = dve.tensor_tensor(out, a, b, op)
                return ins.then_inc(s, 1) if s is not None else ins

            def stt(out, in0, scalar, in1, op0, op1, s):
                ins = dve.scalar_tensor_tensor(out=out, in0=in0, scalar=scalar, in1=in1, op0=op0, op1=op1)
                return ins.then_inc(s, 1) if s is not None else ins

            def copy(out, in_, s):
                ins = dve.tensor_copy(out, in_)
                return ins.then_inc(s, 1) if s is not None else ins

            def fixed():
                dve.wait_ge(ld_con, 48)

            def norm(nk, gcol, split=True, between=lambda c: None, mid=lambda: None):
                for c in range(KC):
                    dve.wait_ge(ss("n_sq"), KC * nk + c + 1)
                    if c == 0:
                        copy(nrm["acc"][:, :], nrm["sq"][:, 0, :], ss("n_acc"))
                    else:
                        dve.wait_ge(ss("n_acc"), KC * nk + c)
                        tt_(nrm["acc"][:, :], nrm["acc"][:, :], nrm["sq"][:, c % 2, :], ALU.add, ss("n_acc"))
                mid()
                dve.wait_ge(ss("n_rt"), nk + 1)
                dve.reciprocal(nrm["rst"][:, :], nrm["rst"][:, :]).then_inc(ss("n_rc"), 1)
                dve.wait_ge(ss("n_rc"), nk + 1)
                if not split:
                    for c in range(KC):
                        stt(X[:, c, :], X[:, c, :], prm[:, gcol + c:gcol + c + 1], nrm["rst"][:, :],
                            ALU.mult, ALU.mult, ss("n_hf"))
                    return

                def lo(c):
                    dve.wait_ge(ss("n_hi"), KC * nk + c + 1)
                    tt_(Hl[:, c, :], nrm["hf"][:, c % 2, :], Hh[:, c, :].bitcast(F32), ALU.subtract, ss("n_lo"))

                for c in range(KC):
                    if c >= 2:
                        dve.wait_ge(ss("n_lo"), KC * nk + c - 1)
                    stt(nrm["hf"][:, c % 2, :], X[:, c, :], prm[:, gcol + c:gcol + c + 1], nrm["rst"][:, :],
                        ALU.mult, ALU.mult, ss("n_hf"))
                    if c:
                        lo(c - 1)
                    between(c)
                lo(KC - 1)

            def add_to_x(t0, bias=None):
                with dve.Fori(0, 4) as i:
                    for s in range(2):
                        dve.wait_ge(tile_done, 2 * i + (t0 + s + 1))
                        xc = X[:, bass.ds(2 * i + s, 1), :].rearrange("p a (g n) -> p (a g) n", g=GRP)
                        if bias is None:
                            tt_(xc, pset(s), xc, ALU.add, set_free[s])
                        else:
                            stt(xc, pset(s), prm[:, bass.ds(2 * i + (bias + s), 1)], xc, ALU.add, ALU.add,
                                set_free[s])

            dve.wait_ge(ld_con, 48)
            norm(0, PCOL["g_mix"])
            with dve.Fori(0, 2) as i:
                for hh in range(2):
                    h = 2 * i + hh
                    dve.wait_ge(tile_done, 6 * i + (T_SB + 3 * hh + 2))
                    copy(grp(sb["sk_"][:, :]), pset(1 - hh), ss("sb_k"))
                    dve.wait_ge(ss("sb_q"), h + 1)
                    fixed()
                    copy(mx["qsel"][:, bass.ds(h, 1), :], sb["sq_"][:, T:N].rearrange(
                        "p (a n) -> p a n", a=1), None)
                    dve.wait_ge(ss("sb_vt"), h + 1)
                    for j in range(2):
                        copy(sb["svt"][:, 4 * j:4 * j + 4, :], ps[:, 6 + j, :].rearrange(
                            "p (c n) -> p c n", c=4), ss("sb_vev"))

                    def score(u):
                        half, j, q0, w = UNITS[u]
                        diag = j >= 4 * half
                        zs = sb["zs"][:, u % 3, :]
                        dve.wait_ge(ss("sb_z"), NU * h + (u + 1))
                        if u >= 3 or hh:
                            dve.wait_ge(ss("sb_ea"), NU * h + (u - 2))
                        dve.tensor_scalar(zs[:, 0:w], ps[:, u % 2, 0:w], SCALE,
                                          prm[:, bass.ds(h + PCOL["sb_bias"], 1)], ALU.mult,
                                          ALU.add).then_inc(ss("sb_zraw" if diag else "sb_zs"), 1)
                        if diag:
                            dve.wait_ge(ss("sb_zraw"), NDIAG * h + (DIAG[u] + 1))
                            tt_(zs[:, 0:P], zs[:, 0:P], lim, ALU.min, ss("sb_zs"))

                    def exponent(u):
                        w = UNITS[u][3]
                        dve.wait_ge(ss("sb_s"), NU * h + (u + 1))
                        if u >= 2 or hh:
                            dve.wait_ge(ss("sb_aa"), NU * h + (u - 1))
                        tt_(sb["ea"][:, u % 2, 0:w], sb["zs"][:, u % 3, 0:w], ps[:, 2 + u % 2, 0:w],
                            ALU.subtract, ss("sb_ea"))

                    def later(u):
                        half, j, q0, w = UNITS[u]
                        cols = slice(q0 - 512 * half, 512)
                        if j == 0:
                            return
                        dve.wait_ge(ss("sb_sp"), NU * h + (u + 1))
                        if j == 4 * half + 3:
                            dve.wait_ge(ss("sb_rr0"), 2 * h + (2 - half))
                            copy(sb["rr"][:, (u + 1) % 2, cols], sb["sp"][:, u % 2, 0:w], ss("sb_rr"))
                        else:
                            dve.wait_ge(ss("sb_rr"), NLATER * h + LATER[u - 1] + 1)
                            tt_(sb["rr"][:, (u + 1) % 2, cols], sb["rr"][:, u % 2, cols],
                                sb["sp"][:, u % 2, 0:w], ALU.add, ss("sb_rr"))

                    score(0)
                    for u in range(NU):
                        half, j, q0, w = UNITS[u]
                        if u + 1 < NU:
                            score(u + 1)
                        dve.wait_ge(ss("sb_lg"), NU * h + (u + 1))
                        stt(sb["sp"][:, u % 2, 0:w], sb["zs"][:, u % 3, 0:w], 0.0, sb["lg"][:, u % 2, 0:w],
                            ALU.max, ALU.add, ss("sb_sp"))
                        if u:
                            exponent(u - 1)
                        if j == 4 * half + 3:
                            if u or hh:
                                dve.wait_ge(ss("sb_rr"), NLATER * h + LATER.get(u - 1, LATER.get(u - 2, -1)) + 1)
                            dve.memset(sb["rr"][:, :, :], 0.0).then_inc(ss("sb_rr0"), 1)
                        later(u)
                    exponent(NU - 1)
                    dve.wait_ge(ss("sb_o"), NU * h + NU)
                    dve.wait_ge(stored, 64 * i + 32 * (hh + 1))
                    fixed()
                    for half in range(2):
                        copy(C[:, bass.ds(h + H, 1), 512 * half:512 * half + 512],
                             ps[:, 6 + half:7 + half, :], ss("sb_oev"))
                end_stage(dve, end_dve, i + 1)
            dve.wait_ge(ss("ld_rope"), 16)
            dve.memset(rt["st"][:, 0, :], 0.0).then_inc(ss("r_st0"), 1)
            dve.memset(rt["zz"][:, 6, 56:64], 0.0).then_inc(ss("r_st0"), 1)
            with dve.Fori(0, H) as i:
                hb = rt["hb"]
                fixed()
                copy(hb[:, :], con[:, bass.ds(HB * i + C_HEAD, HB)], ss("r_hb"))
                fixed()
                copy(rt["selp"][:, :, :], sel[:, bass.ds(2 * i, 2), :], ss("r_selp"))
                half_ = P // 2
                for n, (name, s) in enumerate((("rq", 0), ("rk", 1))):
                    if n:
                        dve.wait_ge(ss("r_q"), i + 1)
                    dve.wait_ge(tile_done, 4 * i + (T_RET + n + 1))
                    tt_(grp(rt["t1"][:, :]), pset(s), grp(rt["cs"][:, 0, :]), ALU.mult, ss("r_rot"))
                    for a, b in ((0, half_), (half_, 0)):
                        ins = dve.tensor_tensor(grp(rt["t2"][a:a + half_, :]), pset(s, b, b + half_),
                                                grp(rt["cs"][b:b + half_, 1, :]), ALU.mult)
                        ins.then_inc(ss("r_rot") if a == 0 else ss("r_qp" if n == 0 else "r_kp"), 1)
                    dve.wait_ge(ss("r_rot"), 4 * i + (2 * n + 2))
                    dve.wait_ge(ss("r_qp" if n == 0 else "r_kp"), i + 1)
                    tt_(rt[name][:, :], rt["t1"][:, :], rt["t2"][:, :], ALU.add,
                        ss("r_q" if n == 0 else "r_k"))
                dve.wait_ge(ss("r_k"), i + 1)
                dve.wait_ge(ss("r_hb"), i + 1)
                tt_(rt["qd"][:, :, :], rt["rq"][:, 0:T].rearrange("p (c n) -> p c n", c=TT),
                    hb[:, P:2 * P].unsqueeze(1).broadcast_to((P, TT, P)), ALU.mult, ss("r_qd"))
                dve.wait_ge(ss("r_kT"), i + 1)
                for j in range(2):
                    dve.tensor_scalar(rt["kt"][:, 4 * j:4 * j + 4, :], ps[:, j, :].rearrange(
                        "p (c n) -> p c n", c=4), hb[:, 2 * P:2 * P + 1], None, ALU.mult)\
                        .then_inc(ss("r_kt"), 1)
                dve.tensor_scalar(rt["kvs"][:, 0, :], ps[0:NS, 2, 0:P], SCALE, None, ALU.mult)\
                    .then_inc(ss("r_kvs"), 1)
                copy(rt["kvs"][:, 1, :], ps[0:NS, 2, P:2 * P], ss("r_kvs"))
                dve.wait_ge(ss("r_kvs"), 2 * i + 2)
                tt_(rt["kms"][:, :, :], rt["kvs"][:, 0:1, :].broadcast_to((NS, NS, P)),
                    con[0:NS, C_ID:C_ID + NS].unsqueeze(2).broadcast_to((NS, NS, P)), ALU.mult, ss("r_kms"))
                dve.wait_ge(ss("r_sc"), i + 1)
                for j in range(2):
                    tt_(rt["sm"][:, 4 * j:4 * j + 4, :], ps[:, 3 + j, :].rearrange("p (c n) -> p c n", c=4),
                        hb[:, 0:P].unsqueeze(1).broadcast_to((P, 4, P)), ALU.mult, ss("r_sm"))
                dve.wait_ge(ss("r_up"), i + 1)
                dve.wait_ge(ss("r_st0"), 2)
                for c in range(TT):
                    if c:
                        dve.wait_ge(ss("r_st"), TT * i + c)
                    stt(rt["st"][:, c + 1, :], rt["st"][:, c, :], hb[:, 2 * P + 1:2 * P + 2],
                        ps[:, c // 4, (c % 4) * P:(c % 4 + 1) * P], ALU.mult, ALU.add, ss("r_st"))
                dve.wait_ge(ss("r_sup"), i + 1)
                dve.wait_ge(ss("ld_s0"), 16 * i + 16)
                for j in range(2):
                    s4 = rt["s0"][:, 4 * j:4 * j + 4, :]
                    stt(s4, s4, hb[:, 2 * P + 2:2 * P + 3], ps[:, 3 + j, :].rearrange(
                        "p (b n) -> p b n", b=4), ALU.mult, ALU.add, ss("r_s1"))
                dve.wait_ge(ss("r_mu"), i + 1)
                stt(grp(rt["t2"][:, :]), pset(0), -1.0 / P, grp(rt["t1"][:, :]), ALU.mult, ALU.add, ss("r_d"))
                dve.wait_ge(ss("r_rt"), i + 1)
                dve.reciprocal(rt["rvT"][:, :], rt["rvT"][:, :]).then_inc(ss("r_rc"), 1)
                dve.wait_ge(ss("r_rc"), i + 1)
                stt(rt["t2"][:, :], rt["t2"][:, :], hb[:, 2 * P + 3:2 * P + 4], rt["rvT"][:, :], ALU.mult,
                    ALU.mult, ss("r_n"))
                dve.wait_ge(ss("r_n"), i + 1)
                tt_(C[:, bass.ds(i, 1), :], rt["t2"][:, :].unsqueeze(1), rt["rg"][:, :].unsqueeze(1),
                    ALU.mult, None)
                z = rt["zz"]
                for n in range(16):
                    b, g = n // PG, n % PG
                    dve.wait_ge(ss(f"ld_k{n % 2}"), 128 * i + 16 * (n // 2 + 1))
                    if g == 0:
                        dve.wait_ge(ss("r_qb"), 2 * i + (b + 1))
                    if n >= 2:
                        dve.wait_ge(kpg_free, 16 * i + (n + 1))
                    for h in range(H):
                        col = g * 8 + b * 4 + h
                        ins = dve.tensor_tensor_reduce(rt["junk"][:, n % 2, h * P:(h + 1) * P], rt["kpg"][:, n % 2, h * P:(h + 1) * P],
                                                       ps[:, 6, h * P:(h + 1) * P], 1.0, 0.0, ALU.mult,
                                                       ALU.add, z[:, 0, col:col + 1])
                    ins.then_inc(kpg_free, 1)
                bias = prm[:, PCOL["sb_bias"]:PCOL["sb_bias"] + H].unsqueeze(1).broadcast_to((P, 16, H))
                dve.wait_ge(kpg_free, 16 * i + 18)
                stt(z[:, 1, :].rearrange("p (a h) -> p a h", h=H), z[:, 0, :].rearrange(
                    "p (a h) -> p a h", h=H), SCALE, bias, ALU.mult, ALU.add, ss("y_z"))
                dve.wait_ge(ss("y_lg"), i + 1)
                stt(z[:, 5, :], z[:, 1, :], 0.0, z[:, 4, :], ALU.max, ALU.add, ss("y_sp"))
                dve.wait_ge(ss("y_sp"), i + 1)
                for g in range(PG - 1, 0, -1):
                    if g < PG - 1:
                        dve.wait_ge(ss("y_r"), 6 * i + (PG - 1 - g))
                    tt_(z[:, 6, 8 * g - 8:8 * g], z[:, 6, 8 * g:8 * g + 8], z[:, 5, 8 * g:8 * g + 8], ALU.add,
                        ss("y_rr") if g == 1 else ss("y_r"))
                dve.wait_ge(ss("y_s"), i + 1)
                tt_(z[:, 7, :], z[:, 1, :], ps[:, 5, 0:64], ALU.subtract, ss("y_ea"))
                dve.wait_ge(vpg_free, 16 * i + 18)
                fixed()
                copy(C[:, H:2 * H, bass.ds(2 * i + T, 2)], ps[:, 7, 0:8].rearrange("p (b h) -> p h b", b=2),
                     ss("y_o"))
                end_stage(dve, end_dve, i + (E_SB + 1))
            for c in range(KC):
                dve.wait_ge(ss("c_hi"), c + 1)
                tt_(Hl[:, c, :], C[:, c, :], Hh[:, c, :].bitcast(F32), ALU.subtract, ss("c_lo"))
            for c in range(KC // 2):
                dve.wait_ge(ld_x[c], 32)
            add_to_x(T_OUT)
            end_stage(dve, end_dve, E_OUT)

            def cross(l, e0, nk, t0, freed):
                def mk(c):
                    dve.wait_ge(*of_layer(l, "mw_used", c + 1))
                    copy(cr["mkT"][:, c, :], ps[:, 3 + c % 3, 0:MEM], ss("mk_ev"))

                norm(nk, PCOL["g_cross"] + KC * l, mid=lambda: [mk(c) for c in range(2)],
                     between=lambda c: mk(c + 2) if c < 6 else None)
                with dve.Fori(0, 4) as i:
                    for s in range(2):
                        dve.wait_ge(tile_done, 2 * i + (t0 + s + 1))
                        dve.tensor_scalar(cr["qx"][:, bass.ds(2 * i + s, 1), :].rearrange(
                            "p a (g n) -> p (a g) n", g=GRP), pset(s), SCALE_X, None, ALU.mult)\
                            .then_inc(set_free[s], 1)
                end_stage(dve, end_dve, e0 + 1)

                def maxima(u):
                    dve.wait_ge(*of_layer(l, "x_s", u + 1))
                    if u >= 2:
                        dve.wait_ge(*of_layer(l, "x_p", u - 1))
                    b = (u % 2) * 2
                    dve.tensor_reduce(at["mst"][:, u % 2, 0, :], ps[:, b:b + 2, :].rearrange(
                        "p b (t m) -> p (b t) m", t=2), AXX, ALU.max, negate=True).then_inc(ss("x_m"), 1)

                def scaled(u):
                    m = at["mst"]
                    dve.wait_ge(*of_layer(l, "x_e", 4 * u + 4))
                    dve.reciprocal(m[:, u % 2, 2, :], m[:, u % 2, 1, :]).then_inc(ss("x_r"), 1)
                    dve.wait_ge(*of_layer(l, "x_r", u + 1))
                    tt_(at["p"][:, u % 2, :, :], at["p"][:, u % 2, :, :],
                        m[:, u % 2, 2, :].unsqueeze(2).broadcast_to((P, 4, MEM)), ALU.mult, ss("x_p"))

                def turned(u):
                    dve.wait_ge(*of_layer(l, "x_t", u + 1))
                    if u >= 2:
                        dve.wait_ge(*of_layer(l, "x_o", 2 * (u - 1)))
                    copy(at["pT"][:, u % 2, 1, :], ps[:, 5, :], ss("x_pt1"))

                def out(u):
                    hx, half = u // 2, u % 2
                    for dc in range(2):
                        dve.wait_ge(*of_layer(l, "x_oh", 2 * u + dc + 1))
                        cols = slice(512 * half, 512 * half + 512)
                        tt_(Hl[:, 2 * hx + dc, cols], ps[:, 6 + dc, :], Hh[:, 2 * hx + dc, cols].bitcast(F32),
                            ALU.subtract, ss("x_ol"))

                maxima(0)
                for u in range(8):
                    if u + 1 < 8:
                        maxima(u + 1)
                    scaled(u)
                    turned(u)
                    if u:
                        out(u - 1)
                out(7)
                end_stage(dve, end_dve, e0 + 2)
                for n in range(NS * MT):
                    b, m = n // MT, n % MT
                    dve.wait_ge(*of_layer(l, f"ld_ck_{n % 2}", 16 * (n // 2 + 1)))
                    if m == 0:
                        dve.wait_ge(*of_layer(l, "xs_qb", b + 1))
                    if n >= 2:
                        dve.wait_ge(*of_layer(l, "ck_used", n - 1))
                    for h in range(H):
                        ins = dve.tensor_tensor_reduce(
                            c3["junk2"][:, n % 2, h * HDX:(h + 1) * HDX], c3["ck"][:, n % 2, h * HDX:(h + 1) * HDX],
                            ps[:, 2 * (b % 2) + h // 2, (h % 2) * HDX:(h % 2 + 1) * HDX], 1.0, 0.0, ALU.mult,
                            ALU.add, c3["zc"][:, m, 4 * b + h:4 * b + h + 1])
                    ins.then_inc(ss("ck_used"), 1)
                dve.wait_ge(*of_layer(l, "xs_t", 1))
                z = c3["zst"]
                dve.tensor_reduce(z[:, 0:1], ps[0:32, 4, 0:MEM], AXX, ALU.max, negate=True)\
                    .then_inc(ss("xs_soft"), 1)
                dve.wait_ge(*of_layer(l, "xs_e", 1))
                dve.reciprocal(z[:, 2:3], z[:, 1:2]).then_inc(ss("xs_soft"), 1)
                dve.wait_ge(*of_layer(l, "xs_soft", 2))
                dve.tensor_scalar(c3["pr"][:, :], c3["pr"][:, :], z[:, 2:3], None, ALU.mult)\
                    .then_inc(ss("xs_soft"), 1)
                dve.wait_ge(*of_layer(l, "xs_t", 2))
                copy(c3["pts"][:, :, :], ps[:, 5, 0:64].rearrange("p (m n) -> p m n", m=MT), ss("xs_soft"))
                dve.wait_ge(*of_layer(l, "xs_oh", 1))
                tt_(Hl[:, :, T:N], ps[:, 6, 0:KC * NS].rearrange("p (c b) -> p c b", c=KC),
                    Hh[:, :, T:N].bitcast(F32), ALU.subtract, None)
                end_stage(dve, end_dve, e0 + 3)
                add_to_x(t0 + 8)
                end_stage(dve, end_dve, e0 + 4)

            def ffn(l, e1, nk, t0, freed):
                dve.memset(ff["ub"][:, :, 0:2], 0.0)
                norm(nk, PCOL["g_ffn"] + KC * l)
                dve.wait_ge(*of_layer(l, "ld_stf", 16))
                fp, ub, cb, gf = ff["fp"], ff["ub"], ff["cb"], ff["gf"]

                def xadd(n, i, t):
                    if n % 4 == 3:
                        dve.wait_ge(tile_done, t + (n // 4 + 1))
                    else:
                        dve.wait_ge(*of_layer(l, "f_dn", 6 * i + (n - n // 4 + 1)))
                    tt_(grp(X[:, n, :]), pset(n % 2), grp(X[:, n, :]), ALU.add, set_free[n % 2])

                def section(i, par, f, between):
                    fixed()
                    copy(fp[:, 0:16], prm[:, bass.ds(16 * i + PCOL[f"ffn{l}"], 16)], None)
                    copy(fp[:, 16:80].rearrange("p (a n) -> p a n", a=1), ff["stf"][:, bass.ds(i, 1), :],
                         ss("f_fp"))
                    dve.wait_ge(*of_layer(l, "f_fp", i + 1))
                    for k in range(2):
                        for v in range(2):
                            q = 2 * k + v
                            c0 = 16 * i + 4 * q
                            dve.wait_ge(set_free[v], f + (k + 2))
                            for tap in range(2):
                                if tap:
                                    dve.wait_ge(*of_layer(l, "f_c", c0 + 1))
                                stt(cb[:, v, 0:T], ub[:, v, tap:tap + T], fp[:, 4 * q + tap:4 * q + tap + 1],
                                    cb[:, v, 0:T], ALU.mult, ALU.add, ss("f_c"))
                                if tap:
                                    dve.wait_ge(*of_layer(l, "f_c", c0 + 2))
                                stt(cb[:, v, T:N], fp[:, 16 + 16 * q + 8 * tap:24 + 16 * q + 8 * tap],
                                    fp[:, 4 * q + tap:4 * q + tap + 1], cb[:, v, T:N], ALU.mult, ALU.add,
                                    ss("f_c"))
                            copy(ff["ftl"][:, 10 * q:10 * q + 10], ub[:, v, T:T + 10], ss("f_ft"))
                        if k:
                            between(0)
                        dve.wait_ge(*of_layer(l, "f_sl", 2 * i + (k + 1)))
                        dve.wait_ge(*of_layer(l, "f_c", 16 * i + (8 * k + 8)))
                        tt_(gf[:, :], cb[:, 0, :], cb[:, 1, :], ALU.mult, ss("f_gm"))
                        if k:
                            between(1)
                        dve.wait_ge(*of_layer(l, "g_hi", 2 * i + (k + 1)))
                        tt_(ff["Gl"][:, par, k, :], gf[:, :], ff["Gh"][:, par, k, :].bitcast(F32),
                            ALU.subtract, ss("g_lo"))
                    dve.wait_ge(*of_layer(l, "f_ft", 4 * i + 4))
                    fixed()
                    copy(ff["tls"][:, bass.ds(i, 1), :], ff["ftl"][:, :].rearrange("p (a n) -> p a n", a=1),
                         ss("f_tl"))
                    for n in range(2, 8):
                        between(n)

                section(0, 0, freed, lambda n: None)
                with dve.Fori(0, SEC // 2) as r:
                    for j in (1, 2):
                        section(2 * r + j, j % 2, 12 * r + (freed + 2 + 6 * (j - 1)),
                                lambda n: xadd(n, 2 * r + (j - 1), 12 * r + (t0 + 8 + 6 * (j - 1))))
                for n in range(8):
                    xadd(n, SEC - 1, t0 + 6 * SEC - 2)
                end_stage(dve, end_dve, e1)

            cross(*CR[0])
            ffn(0, E_FF0, 2, T_FFN0, F_FF0)
            uu, us, cvo, ca, cpar = (cf[x] for x in ("uu", "us", "cvo", "ca", "cpar"))
            dve.memset(uu[:, :, 0:W_CONV - 1], 0.0).then_inc(ss("c_ch"), 1)
            norm(3, PCOL["g_mix"] + KC)
            dve.wait_ge(ss("ld_us"), 16)
            with dve.Fori(0, 4) as i:
                dve.wait_ge(ss("c_ch"), 4 * i + 1)
                fixed()
                copy(cpar[:, :, :], prm[:, bass.ds(2 * CFP * i + PCOL["cf"], 2 * CFP)].rearrange(
                    "p (j n) -> p j n", j=2), ss("c_par"))
                dve.wait_ge(ss("c_par"), i + 1)
                for j in range(2):
                    c = 2 * i + j
                    dve.wait_ge(set_free[1], c + (F_W1 + 2))
                    u = uu[:, j, W_CONV - 1:W_CONV - 1 + N]
                    stt(grp(u), pset(0), cpar[:, j, 0:1], grp(cf["sg"][:, :]), ALU.add, ALU.mult,
                        set_free[0])
                    dve.wait_ge(set_free[0], c + (F_W1 + 2))
                    dve.wait_ge(ss("c_ch"), 4 * i + (2 * j + 1))
                    dve.tensor_scalar(ca[:, 0:T], uu[:, j, 0:T], cpar[:, j, 3:4], cpar[:, j, 2:3], ALU.mult,
                                      ALU.add).then_inc(ss("c_tap"), 1)
                    copy(cf["utl"][:, bass.ds(c, 1), :], uu[:, j, T:T + W_CONV - 1].unsqueeze(1), None)
                    copy(us[:, bass.ds(c, 1), :, W_CONV - 1:W_CONV], u[:, T:N].rearrange(
                        "p (a b n) -> p a b n", a=1, n=1), ss("c_u"))
                    dve.wait_ge(ss("c_u"), c + 1)
                    tt_(cf["usj"][:, :, :].unsqueeze(1), us[:, bass.ds(c, 1), :, :],
                        cpar[:, j, 3:3 + W_CONV].unsqueeze(1).unsqueeze(1).broadcast_to((P, 1, NS, W_CONV)),
                        ALU.mult, ss("c_sm"))
                    dve.wait_ge(ss("c_sm"), c + 1)
                    dve.tensor_reduce(ca[:, T:N], cf["usj"][:, :, :], AXX, ALU.add).then_inc(ss("c_sr"), 1)
                    for w in range(1, W_CONV):
                        dve.wait_ge(ss("c_tap"), 31 * c + w)
                        stt(ca[:, 0:T], uu[:, j, w:w + T], cpar[:, j, 3 + w:4 + w], ca[:, 0:T], ALU.mult,
                            ALU.add, ss("c_tap"))
                    dve.wait_ge(ss("c_sr"), c + 1)
                    dve.wait_ge(ss("c_tap"), 31 * c + W_CONV)
                    fixed()
                    copy(cvo[:, bass.ds(c, 1), 0:T], ca[:, 0:T].unsqueeze(1), ss("c_ch"))
                    dve.tensor_scalar(cvo[:, bass.ds(c, 1), T:N], ca[:, T:N].unsqueeze(1), cpar[:, j, 2:3],
                                      None, ALU.add).then_inc(ss("c_ch"), 1)
            end_stage(dve, end_dve, E_FF0 + 1)
            dve.wait_ge(ss("l_mu"), 1)
            for c in range(KC):
                stt(grp(cvo[:, c, :]), pset(0), -1.0 / D, grp(cvo[:, c, :]), ALU.mult, ALU.add, ss("l_d"))
            dve.wait_ge(ss("l_rt"), 1)
            dve.reciprocal(ln["lrst"][:, :], ln["lrst"][:, :]).then_inc(ss("l_rc"), 1)
            dve.wait_ge(ss("l_rc"), 1)

            def ln_lo(c):
                dve.wait_ge(ss("l_hi"), c + 1)
                tt_(Hl[:, c, :], ln["lhf"][:, c % 2, :], Hh[:, c, :].bitcast(F32), ALU.subtract, ss("l_lo"))

            for c in range(KC):
                if c >= 2:
                    dve.wait_ge(ss("l_lo"), c - 1)
                stt(ln["lhf"][:, c % 2, :], cvo[:, c, :], prm[:, PCOL["ln_g"] + c:PCOL["ln_g"] + c + 1],
                    ln["lrst"][:, :], ALU.mult, ALU.mult, ss("l_hf"))
                if c:
                    ln_lo(c - 1)
            ln_lo(KC - 1)
            add_to_x(T_W2, PCOL["b2"])
            end_stage(dve, end_dve, E_CF)
            cross(*CR[1])
            ffn(1, E_FF1, 5, T_FFN1, F_FF1)
            norm(6, PCOL["g_final"], split=False)


_OUTS = {
    "y": (P, KC, N), "sbk": (H, P, N), "sbv": (H, P, N), "retp": (H, P, P), "rets": (NS, H, P, P),
    "cvp": (P, KC, W_CONV - 1), "cvs": (P, KC, NS, W_CONV), "ffn0": (P, SEC, 40), "ffn1": (P, SEC, 40),
    "st0": (P, SEC, 64), "st1": (P, SEC, 64), "mk": (2, P, KC, MEM), "mv": (2, P, MT, D),
}


def _features(a):
    return np.ascontiguousarray(a.T.reshape(-1, P, a.shape[0]).transpose(1, 0, 2))


def _tiles(w):
    k, m = w.shape
    return w.reshape(k // P, P, m // P, P).transpose(2, 1, 0, 3).reshape(m // P, P, k)


def _wide(w):
    return w.reshape(4, 2, P, 2, 512).transpose(3, 0, 2, 1, 4).reshape(8, P, 1024)


def _inputs(i):
    w_in = _tiles(i["w_in_ab"][0])
    order = [4 * p + h for h in range(H) for p in (4, 5, 6)] + [4 * p + h for h in range(H) for p in range(4)]
    cv1 = _tiles(i["cv_w1"][0])

    def ffn(l):
        up = _tiles(i["ffn_w_up"][l])
        dn = i["ffn_w_down"][l].reshape(SEC, 2, P, 2, 512).transpose(0, 3, 2, 1, 4).reshape(SEC, 2, P, 1024)
        ups = [up[[2 * s, FC + 2 * s, 2 * s + 1, FC + 2 * s + 1]] for s in range(SEC)]
        out = [ups[0]]
        for s in range(1, SEC):
            out += [ups[s], dn[s - 1]]
        return out + [dn[SEC - 1]]

    wts = [w_in[order], _tiles(i["w_out_ab"][0]), _tiles(i["xa_wq"][0]), _tiles(i["xa_wo"][0]), *ffn(0),
           cv1[[j for c in range(KC) for j in (c, KC + c)]], _tiles(i["cv_w2"][0]),
           _tiles(i["xa_wq"][1]), _tiles(i["xa_wo"][1]), *ffn(1)]
    memw = np.concatenate([x for l in range(2) for x in (_tiles(i["xa_wk"][l]), _wide(i["xa_wv"][l]))])

    def cols(a):
        a = np.atleast_2d(a)
        return a.reshape(a.shape[0], -1, P).transpose(2, 0, 1).reshape(P, -1)

    cfp = np.concatenate([i["cv_b1"][0].reshape(2, D), i["cv_dwb"][0][None], i["cv_dw"][0]])
    cfp = cfp.reshape(CFP, KC, P).transpose(2, 1, 0).reshape(P, KC * CFP)

    def section_chunks(a):
        n = a.shape[0]
        return a.reshape(n, 2, SEC, 2, P).transpose(4, 2, 3, 1, 0).reshape(P, SEC, 4, n)

    par = [cols(i["g_mix"]), cols(i["g_cross"]), cols(i["g_ffn"]), cols(i["g_final"]), cols(i["ret_gn_g"]),
           np.broadcast_to(i["sb_bias"], (P, H)), cfp, cols(i["cv_ln_g"]), cols(i["cv_ln_b"]),
           cols(i["cv_b2"])]
    for l in range(2):
        par.append(section_chunks(np.concatenate([i["ffn_dw"][l], i["ffn_dwb"][l][None]])).reshape(P, -1))
    gn = par[4]

    lg = np.log1p(-np.exp2(-5.0 - np.arange(H, dtype=np.float32))).astype(np.float32)
    idx = np.arange(P)
    con = np.zeros((P, NCON), np.float32)
    con[:, C_ID:C_ID + P] = np.eye(P)
    con[:, C_TRI:C_TRI + P] = idx[:, None] >= idx[None, :]
    con[:, C_ONE:C_ONE + P] = 1.0
    con[:, C_LIM:C_LIM + P] = np.where(idx[:, None] < idx[None, :], BIG, -BIG)
    con[:, C_EPS] = EPS
    for h in range(H):
        a = C_HEAD + h * HB
        diff = (idx[None, :] - idx[:, None]).astype(np.float32)
        con[:, a:a + P] = np.where(diff >= 0, np.exp(np.maximum(diff, 0) * lg[h]), 0.0) * SCALE
        con[:, a + P:a + 2 * P] = np.exp((idx + 1).astype(np.float32) * lg[h])[None, :]
        con[:, a + 2 * P] = np.exp((P - 1 - idx).astype(np.float32) * lg[h]) * SCALE
        con[:, a + 2 * P + 1] = np.exp(np.float32(P) * lg[h])
        con[:, a + 2 * P + 2] = np.exp(lg[h])
        con[:, a + 2 * P + 3] = gn[:, h]
    inv = (np.float32(10000.0) ** (-np.arange(64, dtype=np.float32) / np.float32(64))).astype(np.float32)
    pos = np.concatenate([np.arange(T), np.full(NS, PAST)]).astype(np.float32)
    ang = (inv[:, None] * pos[None, :]).astype(np.float32)
    rope = np.stack([np.concatenate([np.cos(ang)] * 2), np.concatenate([np.sin(ang), -np.sin(ang)])], 1)
    selc = np.zeros((NS, NS, P), np.float32)
    selc[np.arange(NS), np.arange(NS)] = 1.0

    def states(l):
        s = i["state_ffn_conv"][l].transpose(1, 0, 2).reshape(2 * NS, 2 * FF)
        return section_chunks(s).reshape(P, SEC, 64)

    return {
        "x": _features(np.concatenate([i["x_prompt"][0], i["x_sample"][:, 0]])),
        "mem": _features(i["mem_prompt"][0]),
        "wts": np.concatenate(wts),
        "memw": memw, "cons": con, "rope": rope.astype(np.float32), "selc": selc,
        "par": np.concatenate(par, 1),
        "stc": i["state_conv"][0].reshape(NS, W_CONV - 1, KC, P).transpose(3, 2, 0, 1),
        "stf0": states(0), "stf1": states(1),
        "stret": i["state_ret"][0].transpose(1, 2, 0, 3),
        "ck": i["cache_sb_k"][0].reshape(NPAGES, P, H * P), "cv": i["cache_sb_v"][0].reshape(NPAGES, P, H * P),
        "cmk": i["cache_mem_k"].reshape(2, NS, MEM, D), "cmv": i["cache_mem_v"].reshape(2, NS, MEM, D),
        "pt": i["page_table"].reshape(1, NS * PG).astype(np.int32),
    }


def _tokens(a):
    return a.transpose(2, 1, 0).reshape(a.shape[2], -1)


def kernel(**inputs):
    from concourse import bacc as _bacc
    from concourse import mybir as _mybir
    from concourse.bass_utils import run_bass_kernel_spmd as _run

    nc = _bacc.Bacc("TRN2", target_bir_lowering=False, num_devices=1)
    arrays, args = {}, []
    for name, a in _inputs({k: np.asarray(v) for k, v in inputs.items()}).items():
        a = np.ascontiguousarray(a)
        arrays[f"in_{name}"] = a
        args.append(nc.dram_tensor(f"in_{name}", a.shape, _mybir.dt.from_np(a.dtype), kind="ExternalInput").ap())
    for name, shape in _OUTS.items():
        args.append(nc.dram_tensor(f"out_{name}", shape, F32, kind="ExternalOutput").ap())
    build(nc, *args)
    r = _run(nc, [arrays], core_ids=[0]).results[0]
    o = {name: np.asarray(r[f"out_{name}"]) for name in _OUTS}

    y = _tokens(o["y"])
    sb = [o[x].transpose(2, 0, 1) for x in ("sbk", "sbv")]

    def taps(l):
        a = o[f"ffn{l}"].reshape(P, SEC, 2, 2, 10)
        return a.transpose(4, 3, 1, 2, 0).reshape(10, 2 * FF)

    def last_state(l):
        a = o[f"st{l}"].reshape(P, SEC, 2, 2, 2, NS)[:, :, :, :, 1]
        return a.transpose(4, 3, 1, 2, 0).reshape(NS, 2 * FF)

    t = [taps(l) for l in range(2)]
    mk = o["mk"].transpose(0, 3, 2, 1).reshape(2, 1, MEM, 4, HDX)
    mv = o["mv"].transpose(0, 2, 1, 3).reshape(2, 1, MEM, 4, HDX)
    out = (
        y[None, :T], y[T:, None],
        sb[0][None, None, :T], sb[1][None, None, :T], sb[0][None, T:, None], sb[1][None, T:, None],
        o["retp"][None, None], o["rets"][None],
        o["cvp"].transpose(2, 1, 0).reshape(1, 1, W_CONV - 1, D),
        o["cvs"][:, :, :, 1:].transpose(2, 3, 1, 0).reshape(1, NS, W_CONV - 1, D),
        np.stack([a[:2] for a in t])[:, None],
        np.stack([np.stack([last_state(l), t[l][2:]], 1) for l in range(2)]),
        mk, mv,
    )
    return tuple(np.ascontiguousarray(a) for a in out)
```

```python
from contextlib import ExitStack

import numpy as np

import concourse.bass as bass
from concourse import mybir

F32 = mybir.dt.float32
F32R = mybir.dt.float32r
I32 = mybir.dt.int32
ALU = mybir.AluOpType
ACT = mybir.ActivationFunctionType
AXX = mybir.AxisListType.X

P = 128
D = 1024
KC = D // P
T = 1024
NS = 8
N = T + NS
GRP = 3
GN = N // GRP
TT = T // P
H = 4
PAST = 1024
PG = PAST // P
NPAGES = 80
MEM = 256
MT = MEM // P
RING = 4
HDX = D // H
FF = 2816
FC = FF // P
SEC = FC // 2
W_CONV = 31
W_PE = 7
W_VE = W_CONV - W_PE
EPS = 1e-6
BIG = 1e30
HD = 128
SCALE = float(HD) ** -0.5
SCALE_X = float(HDX) ** -0.5
UW = T + W_CONV - 1

CFP = 3 + W_CONV
PCOL = {}
_at = 0
for _name, _n in (("g_mix", 2 * KC), ("g_cross", 2 * KC), ("g_ffn", 2 * KC), ("g_final", KC),
                  ("gn", H), ("sb_bias", H), ("cf", KC * CFP), ("ln_g", KC), ("ln_b", KC), ("b2", KC),
                  ("ffn0", SEC * 16), ("ffn1", SEC * 16)):
    PCOL[_name] = _at
    _at += _n
NPAR = _at

C_ID, C_TRI, C_ONE, C_LIM, C_EPS = 0, P, 2 * P, 3 * P, 4 * P
HB = 2 * P + 4
C_HEAD = 4 * P + 4
NCON = C_HEAD + H * HB

T_SB, T_RET, T_OUT = 0, 12, 28
T_WQ0, T_FFN0 = 36, 52
T_W1, T_W2 = 118, 134
T_WQ1, T_FFN1 = 142, 158
NT = 224


def build(nc, x_in, mem_in, wts, memw, cons, rope, selc, par, stc, stf0, stf1, stret,
          cache_k, cache_v, cmk, cmv, ptab,
          y, o_sbk, o_sbv, o_retp, o_rets, o_cvp, o_cvs, o_ffn0, o_ffn1, o_st0, o_st1, o_mk, o_mv):
    with ExitStack() as ctx:
        base_at = nc.sbuf_base + (-nc.sbuf_base) % 64
        top = [base_at]

        def place(name, shape, dt=F32, at=None):
            size = 4 * int(np.prod(shape[1:]))
            size += -size % 32
            if at is None:
                at = top[0]
                top[0] += size
            return nc.alloc_sbuf_tensor_at(name, shape, dt, offset=at), at + size

        def keep(name, shape, dt=F32):
            return place(name, shape, dt)[0]

        where = {}

        def layout(items, at):
            out = {}
            for name, shape, *dt in items:
                where[name] = at
                out[name], at = place(name, shape, *(dt or (F32,)), at)
            assert at <= nc.sbuf_usable_end, (items[0][0], at, nc.sbuf_usable_end)
            return out, at

        def sem(name):
            return ctx.enter_context(nc.semaphore(name))

        x_at = top[0]
        X = keep("X", [P, KC, N])
        Hh = keep("Hh", [P, KC, N], F32R)
        Hl = keep("Hl", [P, KC, N], F32R)
        wraw = keep("wraw", [P, 2, 1024])
        Wh = keep("Wh", [P, 2, 1024], F32R)
        Wl = keep("Wl", [P, 2, 1024], F32R)
        con = keep("con", [P, NCON])
        prm = keep("prm", [P, NPAR])
        sel = keep("sel", [NS, NS, P])
        scr = top[0]
        ident = con[:, C_ID:C_ID + P]
        tri = con[:, C_TRI:C_TRI + P]
        ones = con[:, C_ONE:C_ONE + P]
        lim = con[:, C_LIM:C_LIM + P]
        eps = con[:, C_EPS:C_EPS + 1]
        one = con[:, C_ONE:C_ONE + 1]

        nrm, _ = layout([("sq", [P, 2, N]), ("acc", [P, N]), ("rst", [P, N]), ("hf", [P, 2, N])], scr)
        C, _ = place("C", [P, KC, N], F32, x_at)
        mx, mix_at = layout([("qsel", [P, H, NS]), ("qtok", [NS, H * P])], scr)
        hd, hd_end = layout([("q0", [P, N]), ("k0", [P, N]), ("v0", [P, N])], mix_at)
        sb, _ = layout([("q1", [P, N]), ("k1", [P, N]),
                        ("v1", [P, N]), ("svt", [P, TT, P]), ("zs", [P, 4, 512]), ("lg", [P, 4, 512]),
                        ("sp", [P, 2, 512]), ("rr", [P, 2, 512]), ("ea", [P, 4, 512]),
                        ("aa", [P, 2, 512])], hd_end)
        sb.update(hd)
        rt, _ = layout([("cs", [P, 2, N]), ("rg", [P, N]),
                        ("t1", [P, N]), ("t2", [P, N]), ("vt", [P, TT, P]), ("kt", [P, TT, P]),
                        ("kt_pad", [P, NS]), ("st", [P, TT + 1, P]), ("s0", [P, NS, P]),
                        ("hb", [P, HB]), ("kvs", [NS, 2, P]), ("kms", [NS, NS, P]), ("selp", [NS, 2, P]),
                        ("pg", [P, 2, 2, H * P]), ("qb", [P, 2, H * P]), ("zz", [P, 8, 64]),
                        ("junk", [P, H * P]), ("pt", [1, NS * PG], I32)], hd_end)
        zm = rt["zz"][:, 6:8, :].rearrange("p r (g b h c) -> p (r g) b h c", b=2, h=H, c=2)
        rt.update(rq=hd["q0"], rk=hd["k0"], rvT=hd["v0"])
        rt.update(layout([("rst", [P, N])], where["kt"])[0])
        rt["sm"], rt["qd"] = (rt[x][:, 0:T].rearrange("p (c n) -> p c n", c=TT) for x in ("t1", "t2"))
        cr, cr_at = layout([("qtx", [NS, D]), ("qx", [P, KC, N]), ("mkT", [P, KC, MEM]),
                            ("mv", [P, MT, D])], scr)
        nmem, _ = layout([("memT", [P, KC, MEM]), ("mw", [P, 3, 1024])], cr_at)
        at, _ = layout([("p", [P, 2, 4, MEM]), ("pT", [P, 2, MT, 512]), ("mst", [P, 2, 3, 4])], cr_at)
        c3, _ = layout([("cc", [P, RING, MT, D]), ("zc", [P, MT, 32]),
                        ("zst", [32, 4]), ("pr", [32, MEM]), ("pm", [P, MT * H, NS * NS]), ("ov", [NS, D]),
                        ("junk2", [P, MT, D])], where["qx"])
        cf, _ = layout([("cvo", [P, KC, N]), ("uu", [P, 2, UW + NS]), ("sg", [P, N]),
                            ("us", [P, KC, NS, W_CONV]), ("utl", [P, KC, W_CONV - 1]),
                            ("usj", [P, NS, W_CONV]), ("ca", [P, N]), ("cpar", [P, 2, CFP]),
                            ("dg", [P, 2, W_PE, P])], scr)
        ln, _ = layout([("lsq", [P, 2, N]), ("lrst", [P, N])], where["uu"])
        ln.update(layout([("lhf", [P, 2, N])], where["usj"])[0])
        ff, ff_end = layout([("Gh", [P, 2, 2, N], F32R), ("Gl", [P, 2, 2, N], F32R), ("ub", [P, 2, N + 2]),
                        ("cb", [P, 2, N]), ("gf", [P, N]), ("stf", [P, SEC, 64]), ("tls", [P, SEC, 40]),
                        ("fp", [P, 80]), ("ftl", [P, 40])], scr)
        behind_ffn, _ = layout([("sqf", [P, 2, N]), ("accf", [P, N])], ff_end)
        squares_of = [(behind_ffn["sqf"], behind_ffn["accf"]) if nk in (3, 6) else (nrm["sq"], nrm["acc"])
                      for nk in range(7)]

        ps = ctx.enter_context(nc.psum_tensor("ps", [P, 8, 512], F32))

        def pset(s, p0=0, p1=P):
            return ps[p0:p1, 3 * s:3 * s + 3, 0:GN]

        def grp(row):
            return row.rearrange("p (g n) -> p g n", g=GRP)

        w_raw = [sem("w_raw0"), sem("w_raw1")]
        w_hi = sem("w_hi")
        w_split = sem("w_split")
        tile_done = sem("tile_done")
        set_free = [sem("set_free0"), sem("set_free1")]
        end_pe, end_dve, end_act = sem("end_pe"), sem("end_dve"), sem("end_act")
        ld_con = sem("ld_con")
        ld_x = [sem(f"ld_x{c}") for c in range(KC // 2)]
        stored = sem("stored")
        pg_free = sem("pg_free")
        made = {}

        def ss(name):
            if name not in made:
                made[name] = sem(name)
            return made[name]

        COUNTS = {
            "ld_mem": 16, "ld_mw_0": 96, "ld_mw_1": 80, "ld_mw_2": 80, "mw_used": 16, "mk_ev": KC, "mv_ev": 2,
            "x_qt": 1, "x_qtc": 2, "x_e": 32, "x_s": 8, "x_p": 8, "x_t": 8, "x_pt0": 8, "x_pt1": 8, "x_o": 16,
            "x_oh": 16, "x_ol": 16, "x_m": 8, "x_r": 8, "cc_used": 2 * NS,
            **{f"ld_cc_{s}": 16 * 2 * NS // RING for s in range(RING)}, "xs_qb": NS, "xs_t": 3, "xs_ov": 1,
            "xs_pm": 1, "xs_soft": 5, "xs_e": 1, "xs_oh": 1, "f_dn": 6 * SEC, "g_lo": FC, "g_hi": FC,
            "f_fp": SEC, "f_gm": FC, "f_c": 16 * SEC, "f_sl": FC, "f_ft": 4 * SEC, "f_tl": SEC, "ld_stf": 16,
        }

        def of_layer(l, name, n):
            return ss(name), n + l * COUNTS[name]

        def ended(e, n):
            for s in (end_pe, end_dve, end_act):
                e.wait_ge(s, n)

        def end_stage(e, mine, n):
            e.drain().then_inc(mine, 1)
            ended(e, n)

        E_SB = 2
        E_RET = E_SB + H
        E_OUT = E_RET + 1
        E_CR0 = E_OUT + 4
        E_FF0 = E_CR0 + 1
        E_CF = E_FF0 + 2
        E_CR1 = E_CF + 4
        E_FF1 = E_CR1 + 1

        F_OUT, F_WQ0, F_FF0 = 0, 4, 12
        F_W1 = F_FF0 + 6 * SEC
        F_W2, F_WQ1, F_FF1 = F_W1 + 8, F_W1 + 12, F_W1 + 20
        CR = ((0, E_OUT, 1, T_WQ0, F_WQ0), (1, E_CF, 4, T_WQ1, F_WQ1))

        UNITS = []
        for half in (1, 0):
            for j in range(4 * half + 3, -1, -1):
                q0 = max(512 * half, P * j)
                UNITS.append((half, j, q0, 512 * (half + 1) - q0))
        NU = len(UNITS)
        DIAG = {u: n for n, u in enumerate(u for u, (half, j, _, _) in enumerate(UNITS) if j >= 4 * half)}
        NDIAG = len(DIAG)
        LATER = {u: n for n, u in enumerate(u for u, (_, j, _, _) in enumerate(UNITS) if j)}
        NLATER = len(LATER)

        block = ctx.enter_context(nc.Block())

        @block.sync
        def _(sp):
            def load(dst, src, s):
                sp.dma_start(dst, src).then_inc(s, 16)

            def weight(t, slot, first=False):
                if not first:
                    sp.wait_ge(w_split, t - 1)
                load(wraw[:, slot:slot + 1, :], wts[bass.ds(t, 1)].rearrange("a p n -> p a n"), w_raw[slot])

            def weights(t0, t1):
                with sp.Fori(0, (t1 - t0) // 2) as i:
                    for j in range(2):
                        weight(2 * i + (t0 + j), j)

            def pages(i, m):
                at_pages = [sp.value_load(rt["pt"][0:1, bass.ds(16 * i + (2 * (m % 8) + p), 1)], min_val=0,
                                          max_val=NPAGES - 1) for p in range(2)]
                sp.wait_ge(pg_free, 16 * i + (m + 1))
                for p in range(2):
                    load(rt["pg"][:, m % 2, p:p + 1, :], (cache_k, cache_v)[m // 8][bass.ds(at_pages[p], 1)]
                         .rearrange("a p n -> p a n"), ss(f"ld_pg{m % 2}"))

            def load_x(c):
                load(X[:, 2 * c:2 * c + 2, :], x_in[:, 2 * c:2 * c + 2, :], ld_x[c])

            load_x(0)
            load(con[:, :], cons, ld_con)
            load(prm[:, :], par, ld_con)
            load(sel[:, :, :], selc, ld_con)
            for c in range(1, KC // 2):
                load_x(c)
            for j in range(2):
                weight(j, j, first=True)
            weights(2, T_RET + 6)
            ended(sp, E_SB)
            load(rt["cs"][:, :, :], rope, ss("ld_rope"))
            load(rt["pt"][:, :], ptab, ss("ld_pt"))
            sp.wait_ge(ss("ld_pt"), 16)


            def head(i, more):
                ended(sp, i + E_SB)
                load(rt["s0"][:, :, :], stret[bass.ds(i, 1)].rearrange("h d b e -> d (h b) e"), ss("ld_s0"))
                for m in range(16):
                    pages(i, m)
                    for j, behind in enumerate((1, 1, 9, 9)):
                        if more and m == behind:
                            weight(4 * i + (T_RET + 6 + j), j % 2)

            with sp.Fori(0, H - 1) as i:
                head(i, True)
            head(H - 1, False)
            for c in range(KC // 2):
                sp.wait_ge(ss("c_lo"), 2 * c + 2)
                load_x(c)
            weights(T_OUT + 2, T_WQ0 + 2)

            def cross(l, e0, t0):
                ended(sp, e0)
                load(nmem["memT"][:, :, :], mem_in, ss("ld_mem"))
                for t in range(16):
                    if t >= 3:
                        sp.wait_ge(*of_layer(l, "mw_used", t - 2))
                    load(nmem["mw"][:, t % 3, :], memw[16 * l + t], ss(f"ld_mw_{t % 3}"))
                weights(t0 + 2, t0 + 10)
                ended(sp, e0 + 2)
                for n in range(2 * NS):
                    if n >= RING:
                        sp.wait_ge(*of_layer(l, "cc_used", n - RING + 1))
                    load(c3["cc"][:, n % RING, :, :], (cmk, cmv)[n // NS][l, n % NS].rearrange(
                        "(m p) d -> p m d", p=P), ss(f"ld_cc_{n % RING}"))
                weights(t0 + 10, t0 + 18)

            def ffn(l, e0, t0, t1):
                ended(sp, e0)
                load(ff["stf"][:, :, :], (stf0, stf1)[l], ss("ld_stf"))
                weights(t0 + 2, t1)

            cross(0, E_OUT, T_WQ0)
            ffn(0, E_CR0, T_FFN0, T_W1 + 2)
            ended(sp, E_FF0)
            load(cf["us"][:, :, :, 0:W_CONV - 1], stc, ss("ld_us"))
            weights(T_W1 + 2, T_WQ1 + 2)
            cross(1, E_CF, T_WQ1)
            ffn(1, E_CR1, T_FFN1, NT)

        @block.gpsimd
        def _(pool):
            for s in set_free:
                pool.sem_inc(s, 1)
            pool.sem_inc(pg_free, 2)

            def split(t, j, landed, first=False):
                pool.wait_ge(w_raw[j], landed)
                if not first:
                    pool.wait_ge(tile_done, t - 1)
                pool.tensor_tensor(Wh[:, j, :], wraw[:, j, :], one.broadcast_to((P, 1024)),
                                   ALU.mult).then_inc(w_hi, 1)
                pool.wait_ge(w_hi, t + 1)
                pool.tensor_tensor(Wl[:, j, :], wraw[:, j, :], Wh[:, j, :].bitcast(F32),
                                   ALU.subtract).then_inc(w_split, 1)

            pool.wait_ge(ld_con, 48)
            for j in range(2):
                split(j, j, 16, first=True)
            with pool.Fori(1, NT // 2) as i:
                for j in range(2):
                    split(2 * i + j, j, 16 * i + 16)

        @block.tensor
        def _(pe):
            mm = pe.matmul

            def three(outs, wcol, xs, first, last):
                for a, (w, x) in enumerate(((Wh, 0), (Wh, 1), (Wl, 0))):
                    for o, r in zip(outs, xs[x]):
                        ins = mm(o, w[:, wcol[0], wcol[1]:wcol[1] + P], r,
                                 start=first and a == 0, stop=last and a == 2)
                return ins

            def groups(t, k):
                return [t[:, k, g * GN:(g + 1) * GN] for g in range(GRP)]

            def chunk(slot, s, k):
                ins = three([ps[:, 3 * s + g, 0:GN] for g in range(GRP)], (slot, k * P),
                            (groups(Hh, k), groups(Hl, k)), k == 0, k == KC - 1)
                if k == KC - 1:
                    ins.then_inc(tile_done, 1)

            def tile(t, slot, s):
                pe.wait_ge(w_split, t + 1)
                for k in range(KC):
                    chunk(slot, s, k)

            def first_pair(t, ready):
                behind = KC // 2
                pe.wait_ge(w_split, t + 2)
                for k in range(KC + behind):
                    if k < KC:
                        ready(k)
                        chunk(0, 0, k)
                    if k >= behind:
                        chunk(1, 1, k - behind)

            def product(t0, npairs, freed, ready):
                for s in range(2):
                    pe.wait_ge(set_free[s], freed + 1)
                first_pair(t0, ready)
                with pe.Fori(1, npairs) as i:
                    for s in range(2):
                        pe.wait_ge(set_free[s], i + (freed + 1))
                        tile(2 * i + (t0 + s), s, s)

            def column_sums(src, s, done):
                for g in range(GRP):
                    ins = mm(ps[:, 3 * s + g, 0:GN], ones, src[:, g * GN:(g + 1) * GN], start=True, stop=True)
                ins.then_inc(done, 1)

            def norm_sum(nk):
                pe.wait_ge(ss("n_acc"), KC * (nk + 1))
                column_sums(squares_of[nk][1], 0, ss("n_sum"))

            def split_ready(nk):
                return lambda k: pe.wait_ge(ss("n_lo"), KC * nk + k + 1)

            pe.wait_ge(ld_con, 48)
            norm_sum(0)
            first_pair(T_SB, split_ready(0))
            pe.wait_ge(ss("sb_ev"), 1)
            tile(T_SB + 2, 0, 0)
            with pe.Fori(0, 2) as i:
                for hh in range(2):
                    h = 2 * i + hh
                    q, k_, vT = (sb[f"{x}{hh}"] for x in "qkv")
                    pe.wait_ge(ss("sb_ev"), 3 * h + 3)
                    if hh:
                        pe.wait_ge(ss("sb_oev"), 2 * h)
                    for c in range(TT):
                        ins = pe.transpose(ps[:, 6 + c // 4, (c % 4) * P:(c % 4 + 1) * P],
                                           vT[:, c * P:(c + 1) * P], ident)
                    ins.then_inc(ss("sb_vt"), 1)

                    def scores(u):
                        half, j, q0, w = UNITS[u]
                        if u >= 2 or hh:
                            pe.wait_ge(ss("sb_zs"), NU * h + (u - 1))
                        mm(ps[:, 3 + u % 2, 0:w], k_[:, j * P:(j + 1) * P], q[:, q0:q0 + w],
                           start=True, stop=True).then_inc(ss("sb_z"), 1)

                    def sums(u):
                        half, j, q0, w = UNITS[u]
                        lone = j == 4 * half + 3
                        pe.wait_ge(ss("sb_sp"), NU * h + (u + 1))
                        if u >= 1 or hh:
                            pe.wait_ge(ss("sb_ea"), NU * h + u)
                        ins = mm(ps[:, 5, 0:w], tri, sb["sp"][:, u % 2, 0:w], start=True, stop=lone)
                        if not lone:
                            pe.wait_ge(ss("sb_rr"), NLATER * h + LATER[u - 1] + 1)
                            ins = mm(ps[:, 5, 0:w], ones, sb["rr"][:, u % 2, q0 - 512 * half:512],
                                     start=False, stop=True)
                        ins.then_inc(ss("sb_s"), 1)

                    def values(u):
                        half, j, q0, w = UNITS[u]
                        if u == 0:
                            pe.wait_ge(ss("sb_vev"), 2 * h + 2)
                        pe.wait_ge(ss("sb_aa"), NU * h + (u + 1))
                        mm(ps[:, 6 + half, q0 - 512 * half:512], sb["svt"][:, j, :], sb["aa"][:, u % 2, 0:w],
                           start=j == 4 * half + 3, stop=j == 0, skip_group_check=True).then_inc(ss("sb_o"), 1)

                    def next_chunks(n0, n1):
                        for n in range(n0, n1):
                            j, k = n // KC, n % KC
                            if k == 0:
                                pe.wait_ge(w_split, 6 * i + (T_SB + 3 * hh + 3 + j + 1))
                                pe.wait_ge(ss("sb_ev"), 3 * h + (3 + j))
                            chunk((3 * hh + 3 + j) % 2, 0, k)

                    scores(0)
                    scores(1)
                    for g in range(NU // 2):
                        n = 4 * g
                        if g + 1 < NU // 2:
                            scores(2 * g + 2)
                            scores(2 * g + 3)
                        next_chunks(n, n + 2)
                        sums(2 * g)
                        next_chunks(n + 2, n + 3)
                        sums(2 * g + 1)
                        next_chunks(n + 3, n + 4)
                        if g:
                            values(2 * g - 2)
                            values(2 * g - 1)
                    values(NU - 2)
                    values(NU - 1)
                end_stage(pe, end_pe, i + 1)

            for h in range(H):
                ins = pe.transpose(ps[0:NS, 6, h * P:(h + 1) * P], mx["qsel"][:, h, :], ident)
            ins.then_inc(ss("r_qt"), 1)

            def head(i, more):
                def next_tile(j):
                    if more:
                        pe.wait_ge(ss("r_ev"), 4 * i + (1 + j))
                        tile(4 * i + (T_RET + 4 + j), j % 2, 0)

                pe.wait_ge(ss("r_qtc"), 1)
                pe.wait_ge(ss("r_selp"), i + 1)
                for b in range(2):
                    ins = mm(ps[:, 4 + b, :], rt["selp"][:, b, :], mx["qtok"][:, :], start=True, stop=True)
                ins.then_inc(ss("r_qb"), 1)
                pe.wait_ge(ss("r_ev"), 4 * i + 1)
                for c in range(TT):
                    ins = pe.transpose(ps[:, 6 + c // 4, (c % 4) * P:(c % 4 + 1) * P],
                                       rt["rvT"][:, c * P:(c + 1) * P], ident)
                ins.then_inc(ss("r_vT"), 1)
                next_tile(0)
                pe.wait_ge(ss("r_qbc"), i + 1)
                pe.wait_ge(ss("r_k"), i + 1)
                for c in range(TT):
                    pe.transpose(ps[:, 4 + c // 4, (c % 4) * P:(c % 4 + 1) * P],
                                 rt["rk"][:, c * P:(c + 1) * P], ident)
                pe.transpose(ps[0:NS, 3, 0:P], rt["rk"][:, T:N], ident)
                pe.transpose(ps[0:NS, 3, P:2 * P], rt["rvT"][:, T:N], ident).then_inc(ss("r_kT"), 1)
                pe.wait_ge(ss("r_vt"), 2 * i + 2)
                for c in range(TT):
                    ins = mm(ps[:, 6 + c // 4, (c % 4) * P:(c % 4 + 1) * P], rt["rk"][:, c * P:(c + 1) * P],
                             rt["rq"][:, c * P:(c + 1) * P], start=True, stop=True)
                ins.then_inc(ss("r_sc"), 1)
                next_tile(1)
                pe.wait_ge(ss("r_kt"), 2 * i + 2)
                for c in range(TT):
                    ins = mm(ps[:, 4 + c // 4, (c % 4) * P:(c % 4 + 1) * P], rt["kt"][:, c, :],
                             rt["vt"][:, c, :], start=True, stop=True)
                ins.then_inc(ss("r_up"), 1)
                pe.wait_ge(ss("r_sm"), 2 * i + 2)
                pe.wait_ge(ss("r_kms"), i + 1)
                for b in range(NS):
                    ins = mm(ps[:, 6 + b // 4, (b % 4) * P:(b % 4 + 1) * P], rt["kms"][:, b, :],
                             rt["kvs"][:, 1, :], start=True, stop=True)
                ins.then_inc(ss("r_sup"), 1)
                next_tile(2)
                pe.wait_ge(ss("r_st"), TT * i + TT)
                pe.wait_ge(ss("r_qd"), i + 1)
                for c in range(TT):
                    o = ps[:, 4 + c // 4, (c % 4) * P:(c % 4 + 1) * P]
                    mm(o, rt["vt"][:, c, :], rt["sm"][:, c, :], start=True, stop=False)
                    mm(o, rt["st"][:, c, :], rt["qd"][:, c, :], start=False, stop=True)
                pe.wait_ge(ss("r_s1"), 2 * i + 2)
                for b in range(NS):
                    ins = mm(ps[:, 3, 256 + b:257 + b], rt["s0"][:, b, :], rt["rq"][:, T + b:T + b + 1],
                             start=True, stop=True)
                ins.then_inc(ss("r_o"), 1)
                pe.wait_ge(ss("y_sp"), i + 1)
                pe.wait_ge(ss("y_rr"), i + 1)
                mm(ps[:, 6, 0:64], tri, rt["zz"][:, 4, :], start=True, stop=False)
                mm(ps[:, 6, 0:64], ones, rt["zz"][:, 5, :], start=False, stop=True).then_inc(ss("y_s"), 1)
                pe.wait_ge(ss("r_of"), 2 * i + 2)
                column_sums(rt["t1"], 1, ss("r_mu"))

                def page_values(m):
                    pe.wait_ge(ss(f"ld_pg{m % 2}"), 256 * i + 32 * (4 + m // 2 + 1))
                    for n in (2 * m, 2 * m + 1):
                        b, g = n // PG, n % PG
                        for h in range(H):
                            ins = mm(ps[0:2, 7, h * P:(h + 1) * P], zm[:, g, b, h, :],
                                     rt["pg"][:, m % 2, n % 2, h * P:(h + 1) * P],
                                     start=(n == 0 and h == 0), stop=(n == 15 and h == H - 1),
                                     skip_group_check=True)
                    ins.then_inc(pg_free, 1)

                pe.wait_ge(ss("y_a"), 2 * i + 2)
                for m in range(4):
                    page_values(m)
                next_tile(3)
                pe.wait_ge(ss("r_dsq"), i + 1)
                column_sums(rt["t1"], 1, ss("r_var"))
                for m in range(4, 8):
                    page_values(m)
                pe.wait_ge(ss("y_oc"), i + 1)
                for h in range(H):
                    ins = mm(ps[:, 6, 2 * h:2 * h + 2], rt["junk"][0:2, h * P:(h + 1) * P],
                             con[0:2, C_ID:C_ID + 2], start=True, stop=True)
                ins.then_inc(ss("y_ot"), 1)
                end_stage(pe, end_pe, i + (E_SB + 1))

            tile(T_RET + 3, 1, 0)
            with pe.Fori(0, H - 1) as i:
                head(i, True)
            head(H - 1, False)

            product(T_OUT, 4, F_OUT, lambda k: pe.wait_ge(ss("c_lo"), k + 1))
            end_stage(pe, end_pe, E_OUT)

            def cross(l, e0, nk, t0, freed):
                norm_sum(nk)
                pe.wait_ge(*of_layer(l, "ld_mem", 16))
                for c in range(KC):
                    pe.wait_ge(*of_layer(l, f"ld_mw_{c % 3}", 16 * (c // 3 + 1)))
                    if c >= 3:
                        pe.wait_ge(*of_layer(l, "mk_ev", c - 2))
                    for k in range(KC):
                        ins = mm(ps[:, 3 + c % 3, 0:MEM], nmem["mw"][:, c % 3, k * P:(k + 1) * P],
                                 nmem["memT"][:, k, :], start=k == 0, stop=k == KC - 1)
                    ins.then_inc(ss("mw_used"), 1)
                for t in range(8, 16):
                    half, kk = (t - 8) // 4, (t - 8) % 4
                    pe.wait_ge(*of_layer(l, f"ld_mw_{t % 3}", 16 * (t // 3 + 1)))
                    if half and kk == 0:
                        pe.wait_ge(*of_layer(l, "mv_ev", 1))
                    for k in range(2):
                        for m in range(MT):
                            ins = mm(ps[:, 6 + m, :], nmem["memT"][:, 2 * kk + k, m * P:(m + 1) * P],
                                     nmem["mw"][:, t % 3, k * 512:(k + 1) * 512],
                                     start=(kk == 0 and k == 0), stop=(kk == 3 and k == 1))
                    ins.then_inc(ss("mw_used"), 1)
                pe.wait_ge(*of_layer(l, "mk_ev", KC))
                product(t0, 4, freed, split_ready(nk))
                end_stage(pe, end_pe, e0 + 1)
                for c in range(KC):
                    ins = pe.transpose(ps[0:NS, 6 + c // 4, (c % 4) * P:(c % 4 + 1) * P],
                                       cr["qx"][:, c, T:N], ident)
                ins.then_inc(ss("x_qt"), 1)

                def scores(u):
                    hx, half = u // 2, u % 2
                    if u >= 2:
                        pe.wait_ge(*of_layer(l, "x_e", 4 * (u - 1)))
                    for tt in range(4):
                        for dc in range(2):
                            ins = mm(ps[:, (u % 2) * 2 + tt // 2, (tt % 2) * MEM:(tt % 2 + 1) * MEM],
                                     cr["qx"][:, 2 * hx + dc, (4 * half + tt) * P:(4 * half + tt + 1) * P],
                                     cr["mkT"][:, 2 * hx + dc, :], start=dc == 0, stop=dc == 1)
                    ins.then_inc(ss("x_s"), 1)

                def turn(u):
                    pe.wait_ge(*of_layer(l, "x_p", u + 1))
                    if u:
                        pe.wait_ge(*of_layer(l, "x_pt0", u))
                        pe.wait_ge(*of_layer(l, "x_pt1", u))
                    for m in range(MT):
                        for tt in range(4):
                            ins = pe.transpose(ps[:, 4 + m, tt * P:(tt + 1) * P],
                                               at["p"][:, u % 2, tt, m * P:(m + 1) * P], ident)
                    ins.then_inc(ss("x_t"), 1)

                def weigh(u):
                    hx = u // 2
                    pe.wait_ge(*of_layer(l, "x_pt0", u + 1))
                    pe.wait_ge(*of_layer(l, "x_pt1", u + 1))
                    if u == 0:
                        pe.wait_ge(*of_layer(l, "x_qtc", 2))
                    else:
                        pe.wait_ge(*of_layer(l, "x_ol", 2 * u))
                    for dc in range(2):
                        for m in range(MT):
                            ins = mm(ps[:, 6 + dc, :], cr["mv"][:, m, (2 * hx + dc) * P:(2 * hx + dc + 1) * P],
                                     at["pT"][:, u % 2, m, :], start=m == 0, stop=m == MT - 1)
                        ins.then_inc(ss("x_o"), 1)

                scores(0)
                for u in range(8):
                    if u + 1 < 8:
                        scores(u + 1)
                    turn(u)
                    if u:
                        weigh(u - 1)
                weigh(7)
                end_stage(pe, end_pe, e0 + 2)
                for b in range(NS):
                    if b >= 2:
                        pe.wait_ge(*of_layer(l, "cc_used", b - 1))
                    for j in range(2):
                        ins = mm(ps[:, 2 * (b % 2) + j, :], sel[:, b, :], cr["qtx"][:, j * 512:(j + 1) * 512],
                                 start=True, stop=True)
                    ins.then_inc(ss("xs_qb"), 1)
                pe.wait_ge(*of_layer(l, "cc_used", NS))
                for m in range(MT):
                    ins = pe.transpose(ps[0:32, 4, m * P:(m + 1) * P], c3["zc"][:, m, :], ident)
                ins.then_inc(ss("xs_t"), 1)
                pe.wait_ge(*of_layer(l, "xs_soft", 3))
                for m in range(MT):
                    ins = pe.transpose(ps[:, 5, m * 32:(m + 1) * 32], c3["pr"][:, m * P:(m + 1) * P],
                                       con[0:32, C_ID:C_ID + 32])
                ins.then_inc(ss("xs_t"), 1)
                pe.wait_ge(*of_layer(l, "xs_soft", 5))
                for b in range(NS):
                    n = NS + b
                    pe.wait_ge(*of_layer(l, f"ld_cc_{n % RING}", 16 * (n // RING + 1)))
                    for m in range(MT):
                        for h in range(H):
                            ins = mm(ps[0:NS, 6 + h // 2, (h % 2) * HDX:(h % 2 + 1) * HDX],
                                     c3["pm"][:, m * H + h, b * NS:(b + 1) * NS],
                                     c3["cc"][:, n % RING, m, h * HDX:(h + 1) * HDX],
                                     start=(b == 0 and m == 0 and h % 2 == 0),
                                     stop=(b == NS - 1 and m == MT - 1 and h % 2 == 1),
                                     skip_group_check=True)
                    ins.then_inc(ss("cc_used"), 1)
                pe.wait_ge(*of_layer(l, "xs_ov", 1))
                for c in range(KC):
                    ins = pe.transpose(ps[:, 4, c * NS:(c + 1) * NS], c3["ov"][:, c * P:(c + 1) * P],
                                       con[0:NS, C_ID:C_ID + NS])
                ins.then_inc(ss("xs_t"), 1)
                end_stage(pe, end_pe, e0 + 3)
                product(t0 + 8, 4, freed + 4, lambda k: None)
                end_stage(pe, end_pe, e0 + 4)

            def ffn(l, e1, nk, t0, freed):
                norm_sum(nk)

                def up(i, t, f, q0=0):
                    for q in range(q0, 4):
                        pe.wait_ge(set_free[q % 2], f + (q // 2 + 1))
                        tile(t + q, q % 2, q % 2)

                def down(i, par, t, f):
                    pe.wait_ge(*of_layer(l, "g_lo", 2 * i + 2))
                    for n in range(8):
                        if n % 4 == 0:
                            pe.wait_ge(w_split, t + (n // 4 + 1))
                        pe.wait_ge(set_free[n % 2], f + (n // 2 + 1))
                        for kk in range(2):
                            ins = three([ps[:, 3 * (n % 2) + g, 0:GN] for g in range(GRP)],
                                        (n // 4, kk * 512 + (n % 4) * P),
                                        [[G[:, par, kk, g * GN:(g + 1) * GN] for g in range(GRP)]
                                         for G in (ff["Gh"], ff["Gl"])], kk == 0, kk == 1)
                        ins.then_inc(tile_done if n % 4 == 3 else ss("f_dn"), 1)

                for s in range(2):
                    pe.wait_ge(set_free[s], freed + 1)
                first_pair(t0, split_ready(nk))
                up(0, t0, freed, 2)
                with pe.Fori(0, SEC // 2) as r:
                    for j in (1, 2):
                        up(2 * r + j, 12 * r + (t0 + 4 + 6 * (j - 1)), 12 * r + (freed + 2 + 6 * (j - 1)))
                        down(2 * r + (j - 1), (j - 1) % 2, 12 * r + (t0 + 8 + 6 * (j - 1)),
                             12 * r + (freed + 4 + 6 * (j - 1)))
                down(SEC - 1, 0, t0 + 6 * SEC - 2, freed + 6 * SEC - 4)
                end_stage(pe, end_pe, e1)

            cross(*CR[0])
            ffn(0, E_FF0, 2, T_FFN0, F_FF0)
            norm_sum(3)
            def gated(c):
                for s in range(2):
                    pe.wait_ge(set_free[s], c + (F_W1 + 1))
                    tile(2 * c + (T_W1 + s), s, s)

            def last_taps(c, j):
                pe.wait_ge(ss("c_dg"), c + 1)
                pe.wait_ge(set_free[0], c + (F_W1 + 2))
                pe.wait_ge(ss("c_ch"), 2 * c + 1)
                for half in range(2):
                    for n in range(W_PE):
                        a = W_CONV - W_PE + n + 512 * half
                        ins = mm(ps[:, 6 + half, :], cf["dg"][:, j, n, :], cf["uu"][:, j, a:a + 512],
                                 start=n == 0, stop=n == W_PE - 1)
                ins.then_inc(ss("c_pt"), 1)

            for s in range(2):
                pe.wait_ge(set_free[s], F_W1 + 1)
            first_pair(T_W1, split_ready(3))
            with pe.Fori(0, KC // 2 - 1) as i:
                gated(2 * i + 1)
                last_taps(2 * i, 0)
                gated(2 * i + 2)
                last_taps(2 * i + 1, 1)
            gated(KC - 1)
            last_taps(KC - 2, 0)
            last_taps(KC - 1, 1)
            for c in range(KC):
                if c == KC - 1:
                    pe.wait_ge(ss("c_ch"), 2 * KC + 1)
                for g in range(GRP):
                    ins = mm(ps[:, g, 0:GN], ones, cf["cvo"][:, c, g * GN:(g + 1) * GN],
                             start=c == 0, stop=c == KC - 1)
            ins.then_inc(ss("l_mu"), 1)
            end_stage(pe, end_pe, E_FF0 + 1)
            for c in range(KC):
                pe.wait_ge(ss("l_sq"), c + 1)
                for g in range(GRP):
                    ins = mm(ps[:, 3 + g, 0:GN], ones, ln["lsq"][:, c % 2, g * GN:(g + 1) * GN],
                             start=c == 0, stop=c == KC - 1)
                ins.then_inc(ss("l_sqs"), 1)
            product(T_W2, 4, F_W2, lambda k: pe.wait_ge(ss("l_lo"), k + 1))
            end_stage(pe, end_pe, E_CF)
            cross(*CR[1])
            ffn(1, E_FF1, 5, T_FFN1, F_FF1)
            norm_sum(6)

        @block.scalar
        def _(act):
            nstored = [0]

            def store(dst, src, times=1):
                act.dma_start(dst, src).then_inc(stored, 16)
                nstored[0] += times

            def fn(out, in_, f, s, **kw):
                ins = act.activation(out, in_, f, **kw)
                if s is not None:
                    ins.then_inc(s, 1)

            def fixed():
                act.wait_ge(ld_con, 48)

            def square(nk, c):
                if c >= 2:
                    act.wait_ge(ss("n_acc"), KC * nk + c - 1)
                fn(squares_of[nk][0][:, c % 2, :], X[:, c, :], ACT.Square, ss("n_sq"))

            def squares(nk, freed):
                for c in range(KC):
                    act.wait_ge(set_free[c % 2], freed + c // 2 + 2)
                    square(nk, c)

            def norm(nk, hi=True):
                act.wait_ge(ss("n_sum"), nk + 1)
                fn(grp(nrm["rst"][:, :]), pset(0), ACT.Sqrt, ss("n_rt"), scale=1.0 / D, bias=eps)
                if hi:
                    for c in range(KC):
                        act.wait_ge(ss("n_hf"), KC * nk + c + 1)
                        fn(Hh[:, c, :], nrm["hf"][:, c % 2, :], ACT.Copy, ss("n_hi"))

            act.wait_ge(ld_con, 48)
            for c in range(KC):
                act.wait_ge(ld_x[c // 2], 16)
                square(0, c)
            norm(0)
            def sb_evacuate(j, hh, s, done):
                act.wait_ge(tile_done, done)
                fn(grp(sb[f"{'kvq'[j]}{hh}"][:, :]), pset(s), ACT.Copy, ss("sb_ev"))

            for j in range(3):
                sb_evacuate(j, 0, j % 2, T_SB + j + 1)
            with act.Fori(0, 2) as i:
                for hh in range(2):
                    h = 2 * i + hh
                    if hh:
                        act.wait_ge(stored, 64 * i + 32)
                    act.wait_ge(ss("sb_ev"), 3 * h + 3)
                    store(o_sbk[bass.ds(h, 1)].rearrange("h p n -> p (h n)"), sb[f"k{hh}"][:, :], 2)
                    store(o_sbv[bass.ds(h, 1)].rearrange("h p n -> p (h n)"), sb[f"v{hh}"][:, :], 2)

                    def front(g):
                        for u in (2 * g, 2 * g + 1):
                            w = UNITS[u][3]
                            act.wait_ge(ss("sb_zs"), NU * h + (u + 1))
                            if u >= 4 or hh:
                                act.wait_ge(ss("sb_sp"), NU * h + (u - 3))
                            fn(sb["lg"][:, u % 4, 0:w], sb["zs"][:, u % 4, 0:w], ACT.Abs, ss("sb_sp1"))
                        for u in (2 * g, 2 * g + 1):
                            w = UNITS[u][3]
                            act.wait_ge(ss("sb_sp1"), 2 * NU * h + (4 * g + u % 2 + 1))
                            fn(sb["lg"][:, u % 4, 0:w], sb["lg"][:, u % 4, 0:w], ACT.Exp, ss("sb_sp1"),
                               scale=-1.0)

                    def logs(g):
                        for u in (2 * g, 2 * g + 1):
                            w = UNITS[u][3]
                            act.wait_ge(ss("sb_sp1"), 2 * NU * h + (4 * g + u % 2 + 3))
                            fn(sb["lg"][:, u % 4, 0:w], sb["lg"][:, u % 4, 0:w], ACT.Ln, ss("sb_lg"), bias=one)

                    def probs(g):
                        for u in (2 * g, 2 * g + 1):
                            w = UNITS[u][3]
                            act.wait_ge(ss("sb_ea"), NU * h + (u + 1))
                            if u >= 2 or hh:
                                act.wait_ge(ss("sb_o"), NU * h + (u - 1))
                            fn(sb["aa"][:, u % 2, 0:w], sb["ea"][:, u % 4, 0:w], ACT.Exp, ss("sb_aa"))

                    def next_product(j):
                        sb_evacuate(j, 1 - hh, 0, 6 * i + (T_SB + 3 * hh + 3 + j + 1))

                    front(0)
                    for g in range(NU // 2):
                        logs(g)
                        if g in (2, 4):
                            next_product(g // 2 - 1)
                        if g + 1 < NU // 2:
                            front(g + 1)
                        if g:
                            probs(g - 1)
                    next_product(2)
                    if hh:
                        act.wait_ge(stored, 64 * i + 64)
                    probs(NU // 2 - 1)
                end_stage(act, end_act, i + 1)
            act.wait_ge(ss("r_qt"), 1)
            fn(mx["qtok"][:, :], ps[0:NS, 6, :], ACT.Copy, ss("r_qtc"))
            def evacuate(j, done):
                act.wait_ge(tile_done, done)
                fn(grp(rt[("rk", "rvT", "rq", "rg")[j]][:, :]), pset(0), ACT.Silu if j == 3 else ACT.Copy,
                   ss("r_ev"))

            def head(i, more):
                act.wait_ge(ss("r_qb"), i + 1)
                fn(rt["qb"][:, :, :], ps[:, 4:6, :], ACT.Copy, ss("r_qbc"))
                act.wait_ge(ss("r_vT"), i + 1)
                for j in range(2):
                    fn(rt["vt"][:, 4 * j:4 * j + 4, :], ps[:, 6 + j, :].rearrange("p (c n) -> p c n", c=4),
                       ACT.Copy, ss("r_vt"))
                if more:
                    act.wait_ge(ss("r_sc"), i + 1)
                    evacuate(0, 4 * i + (T_RET + 5))
                    evacuate(1, 4 * i + (T_RET + 6))
                z = rt["zz"]
                act.wait_ge(ss("y_z"), i + 1)
                fn(z[:, 2, :], z[:, 1, :], ACT.Abs, ss("y_sp1"))
                act.wait_ge(ss("y_sp1"), 2 * i + 1)
                fn(z[:, 2, :], z[:, 2, :], ACT.Exp, ss("y_sp1"), scale=-1.0)
                act.wait_ge(ss("y_sp1"), 2 * i + 2)
                fn(z[:, 2, :], z[:, 2, :], ACT.Ln, ss("y_lg"), bias=one)
                act.wait_ge(ss("r_o"), i + 1)
                fn(rt["t1"][:, 0:T].rearrange("p (j n) -> p j n", j=2), ps[:, 4:6, :], ACT.Copy, ss("r_of"))
                fn(rt["t1"][:, T:N], ps[:, 3, 256:256 + NS], ACT.Copy, ss("r_of"))
                if more:
                    evacuate(2, 4 * i + (T_RET + 7))
                act.wait_ge(ss("y_ea"), i + 1)
                for b in range(2):
                    fn(zm[:, :, b, :, b], z[:, 3, :].rearrange("p (g b h) -> p g b h", b=2, h=H)[:, :, b, :],
                       ACT.Exp, ss("y_a"))
                act.wait_ge(ss("r_d"), i + 1)
                fn(rt["t1"][:, :], rt["t2"][:, :], ACT.Square, ss("r_dsq"))
                store(o_retp[bass.ds(i, 1)].rearrange("h d e -> d (h e)"), rt["st"][:, TT, :],
                      H - 1 if more else 1)
                store(o_rets[:, bass.ds(i, 1)].rearrange("b h d e -> d (b h) e"), rt["s0"][:, :, :],
                      H - 1 if more else 1)
                act.wait_ge(ss("r_var"), i + 1)
                fn(grp(rt["rst"][:, :]), pset(1), ACT.Sqrt, ss("r_rt"), scale=1.0 / P, bias=eps)
                act.wait_ge(pg_free, 16 * i + 18)
                act.wait_ge(stored, 32 * i + (16 * 8 + 32))
                fn(rt["junk"][0:2, :], ps[0:2, 7, :], ACT.Copy, ss("y_oc"))
                if more:
                    act.wait_ge(ss("r_c"), i + 1)
                    evacuate(3, 4 * i + (T_RET + 8))
                end_stage(act, end_act, i + (E_SB + 1))

            evacuate(3, T_RET + 4)
            with act.Fori(0, H - 1) as i:
                head(i, True)
            head(H - 1, False)
            for c in range(KC):
                fn(Hh[:, c, :], C[:, c, :], ACT.Copy, ss("c_hi"))
            squares(1, F_OUT)
            end_stage(act, end_act, E_OUT)

            def cross(l, e0, nk, t0, freed):
                norm(nk)
                for half in range(2):
                    act.wait_ge(*of_layer(l, "mw_used", 8 + 4 * (half + 1)))
                    fn(cr["mv"][:, :, half * 512:(half + 1) * 512], ps[:, 6:8, :], ACT.Copy, ss("mv_ev"))
                act.wait_ge(*of_layer(l, "mk_ev", KC))
                store(o_mk[l], cr["mkT"][:, :, :])
                act.wait_ge(*of_layer(l, "mv_ev", 2))
                store(o_mv[l], cr["mv"][:, :, :])
                end_stage(act, end_act, e0 + 1)
                act.wait_ge(*of_layer(l, "x_qt", 1))
                for j in range(2):
                    fn(cr["qtx"][:, j * 512:(j + 1) * 512], ps[0:NS, 6 + j, :], ACT.Copy, ss("x_qtc"))

                def exps(u):
                    act.wait_ge(*of_layer(l, "x_m", u + 1))
                    if u >= 2:
                        act.wait_ge(*of_layer(l, "x_t", u - 1))
                    for tt in range(4):
                        fn(at["p"][:, u % 2, tt, :],
                           ps[:, (u % 2) * 2 + tt // 2, (tt % 2) * MEM:(tt % 2 + 1) * MEM], ACT.Exp,
                           ss("x_e"), bias=at["mst"][:, u % 2, 0, tt:tt + 1],
                           accum_out=at["mst"][:, u % 2, 1, tt:tt + 1])

                def turned(u):
                    act.wait_ge(*of_layer(l, "x_t", u + 1))
                    if u >= 2:
                        act.wait_ge(*of_layer(l, "x_o", 2 * (u - 1)))
                    fn(at["pT"][:, u % 2, 0, :], ps[:, 4, :], ACT.Copy, ss("x_pt0"))

                def out(u):
                    hx, half = u // 2, u % 2
                    for dc in range(2):
                        act.wait_ge(*of_layer(l, "x_o", 2 * u + dc + 1))
                        fn(Hh[:, 2 * hx + dc, 512 * half:512 * half + 512], ps[:, 6 + dc, :], ACT.Copy,
                           ss("x_oh"))

                exps(0)
                for u in range(8):
                    if u + 1 < 8:
                        exps(u + 1)
                    turned(u)
                    if u:
                        out(u - 1)
                out(7)
                act.wait_ge(stored, 16 * nstored[0])
                end_stage(act, end_act, e0 + 2)
                act.wait_ge(*of_layer(l, "xs_soft", 1))
                fn(c3["pr"][:, :], ps[0:32, 4, 0:MEM], ACT.Exp, ss("xs_e"), bias=c3["zst"][:, 0:1],
                   accum_out=c3["zst"][:, 1:2])
                act.wait_ge(*of_layer(l, "cc_used", 2 * NS))
                fn(c3["ov"][:, :].rearrange("b (j n) -> b j n", j=2), ps[0:NS, 6:8, :], ACT.Copy, ss("xs_ov"))
                act.wait_ge(*of_layer(l, "xs_t", 3))
                fn(Hh[:, :, T:N], ps[:, 4, 0:KC * NS].rearrange("p (c b) -> p c b", c=KC), ACT.Copy,
                   ss("xs_oh"))
                end_stage(act, end_act, e0 + 3)
                squares(nk + 1, freed + 4)
                end_stage(act, end_act, e0 + 4)

            def ffn(l, e1, nk, t0, freed):
                norm(nk)

                def pair(i, k, par, t, first):
                    for v in range(2):
                        q = 2 * k + v
                        if v == 0:
                            act.wait_ge(*of_layer(l, "f_fp", i + 1))
                            if not first:
                                act.wait_ge(*of_layer(l, "f_gm", 2 * i + k))
                        act.wait_ge(tile_done, t + (v + 1))
                        fn(grp(ff["ub"][:, v, 2:N + 2]), pset(v), ACT.Copy, None)
                        fn(grp(ff["cb"][:, v, :]), pset(v), ACT.Identity, set_free[v],
                           scale=ff["fp"][:, 4 * q + 2:4 * q + 3], bias=ff["fp"][:, 4 * q + 3:4 * q + 4])
                        if v == 0:
                            act.wait_ge(*of_layer(l, "f_c", 16 * i + (4 * q + 4)))
                            fn(ff["cb"][:, 0, :], ff["cb"][:, 0, :], ACT.Silu, ss("f_sl"))
                    act.wait_ge(*of_layer(l, "f_gm", 2 * i + (k + 1)))
                    if not isinstance(i, int):
                        act.wait_ge(tile_done, 6 * i + (t0 - 2))
                    fn(ff["Gh"][:, par, k, :], ff["gf"][:, :], ACT.Copy, ss("g_hi"))

                pair(0, 0, 0, t0, True)
                pair(0, 1, 0, t0 + 2, False)
                with act.Fori(0, SEC // 2) as r:
                    for j in (1, 2):
                        for k in range(2):
                            pair(2 * r + j, k, j % 2, 12 * r + (t0 + 4 + 6 * (j - 1) + 2 * k), False)
                act.wait_ge(*of_layer(l, "f_tl", SEC))
                store((o_ffn0, o_ffn1)[l], ff["tls"][:, :, :])
                store((o_st0, o_st1)[l], ff["stf"][:, :, :])
                squares(nk + 1, freed + 6 * SEC - 4)
                act.wait_ge(stored, 16 * nstored[0])
                end_stage(act, end_act, e1)

            cross(*CR[0])
            ffn(0, E_FF0, 2, T_FFN0, F_FF0)
            norm(3)
            with act.Fori(0, KC // 2) as i:
                for j in range(2):
                    act.wait_ge(ss("c_par"), 2 * i + (j + 1))
                    act.wait_ge(tile_done, 4 * i + (T_W1 + 2 * j + 2))
                    act.wait_ge(set_free[0], 2 * i + (F_W1 + 1 + j))
                    fn(grp(cf["sg"][:, :]), pset(1), ACT.Sigmoid, set_free[1], bias=cf["cpar"][:, j, 1:2])
                    for n in range(W_PE):
                        a = 3 + W_CONV - W_PE + n
                        fn(cf["dg"][:, j, n, :], ident, ACT.Identity, ss("c_dg") if n == W_PE - 1 else None,
                           scale=cf["cpar"][:, j, a:a + 1])
            end_stage(act, end_act, E_FF0 + 1)
            store(o_cvp, cf["utl"][:, :, :])
            store(o_cvs, cf["us"][:, :, :, :])
            for c in range(KC):
                act.wait_ge(ss("l_d"), c + 1)
                if c >= 2:
                    act.wait_ge(ss("l_sqs"), c - 1)
                fn(ln["lsq"][:, c % 2, :], cf["cvo"][:, c, :], ACT.Square, ss("l_sq"))
            act.wait_ge(ss("l_sqs"), KC)
            fn(grp(ln["lrst"][:, :]), pset(1), ACT.Sqrt, ss("l_rt"), scale=1.0 / D, bias=eps)
            for c in range(KC):
                act.wait_ge(ss("l_hf"), c + 1)
                fn(ln["lhf"][:, c % 2, :], ln["lhf"][:, c % 2, :], ACT.Silu, ss("l_si"),
                   bias=prm[:, PCOL["ln_b"] + c:PCOL["ln_b"] + c + 1])
                act.wait_ge(ss("l_si"), c + 1)
                fn(Hh[:, c, :], ln["lhf"][:, c % 2, :], ACT.Copy, ss("l_hi"))
            squares(4, F_W2)
            act.wait_ge(stored, 16 * nstored[0])
            end_stage(act, end_act, E_CF)
            cross(*CR[1])
            ffn(1, E_FF1, 5, T_FFN1, F_FF1)
            norm(6, hi=False)
            for c in range(KC):
                act.wait_ge(ss("n_hf"), KC * 6 + c + 1)
                store(y[:, c, :], X[:, c, :])
            act.wait_ge(stored, 16 * nstored[0])

        @block.vector
        def _(dve):
            def tt_(out, a, b, op, s):
                ins = dve.tensor_tensor(out, a, b, op)
                return ins.then_inc(s, 1) if s is not None else ins

            def stt(out, in0, scalar, in1, op0, op1, s):
                ins = dve.scalar_tensor_tensor(out=out, in0=in0, scalar=scalar, in1=in1, op0=op0, op1=op1)
                return ins.then_inc(s, 1) if s is not None else ins

            def copy(out, in_, s):
                ins = dve.tensor_copy(out, in_)
                return ins.then_inc(s, 1) if s is not None else ins

            def fixed():
                dve.wait_ge(ld_con, 48)

            def sum_square(nk, c):
                sq, acc = squares_of[nk]
                dve.wait_ge(ss("n_sq"), KC * nk + c + 1)
                if c == 0:
                    copy(acc[:, :], sq[:, 0, :], ss("n_acc"))
                else:
                    dve.wait_ge(ss("n_acc"), KC * nk + c)
                    tt_(acc[:, :], acc[:, :], sq[:, c % 2, :], ALU.add, ss("n_acc"))

            def norm(nk, gcol, split=True, between=lambda c: None):
                dve.wait_ge(ss("n_rt"), nk + 1)
                dve.reciprocal(nrm["rst"][:, :], nrm["rst"][:, :]).then_inc(ss("n_rc"), 1)
                dve.wait_ge(ss("n_rc"), nk + 1)
                if not split:
                    for c in range(KC):
                        stt(X[:, c, :], X[:, c, :], prm[:, gcol + c:gcol + c + 1], nrm["rst"][:, :],
                            ALU.mult, ALU.mult, ss("n_hf"))
                    return

                def lo(c):
                    dve.wait_ge(ss("n_hi"), KC * nk + c + 1)
                    tt_(Hl[:, c, :], nrm["hf"][:, c % 2, :], Hh[:, c, :].bitcast(F32), ALU.subtract, ss("n_lo"))

                for c in range(KC):
                    if c >= 2:
                        dve.wait_ge(ss("n_lo"), KC * nk + c - 1)
                    stt(nrm["hf"][:, c % 2, :], X[:, c, :], prm[:, gcol + c:gcol + c + 1], nrm["rst"][:, :],
                        ALU.mult, ALU.mult, ss("n_hf"))
                    if c:
                        lo(c - 1)
                    between(c)
                lo(KC - 1)

            def add_to_x(t0, nk, bias=None):
                for c in range(KC):
                    dve.wait_ge(tile_done, t0 + c + 1)
                    xc = grp(X[:, c, :])
                    if bias is None:
                        tt_(xc, pset(c % 2), xc, ALU.add, set_free[c % 2])
                    else:
                        stt(xc, pset(c % 2), prm[:, bias + c:bias + c + 1], xc, ALU.add, ALU.add,
                            set_free[c % 2])
                    if c:
                        sum_square(nk, c - 1)
                sum_square(nk, KC - 1)

            dve.wait_ge(ld_con, 48)
            for c in range(KC):
                sum_square(0, c)
            norm(0, PCOL["g_mix"])
            with dve.Fori(0, 2) as i:
                for hh in range(2):
                    h = 2 * i + hh
                    dve.wait_ge(ss("sb_ev"), 3 * h + 3)
                    fixed()
                    copy(mx["qsel"][:, bass.ds(h, 1), :], sb[f"q{hh}"][:, T:N].rearrange(
                        "p (a n) -> p a n", a=1), None)
                    dve.wait_ge(ss("sb_vt"), h + 1)
                    for j in range(2):
                        copy(sb["svt"][:, 4 * j:4 * j + 4, :], ps[:, 6 + j, :].rearrange(
                            "p (c n) -> p c n", c=4), ss("sb_vev"))

                    def score(u):
                        half, j, q0, w = UNITS[u]
                        diag = j >= 4 * half
                        zs = sb["zs"][:, u % 4, :]
                        dve.wait_ge(ss("sb_z"), NU * h + (u + 1))
                        if u >= 4 or hh:
                            dve.wait_ge(ss("sb_ea"), NU * h + (u - 3))
                        dve.tensor_scalar(zs[:, 0:w], ps[:, 3 + u % 2, 0:w], SCALE,
                                          prm[:, bass.ds(h + PCOL["sb_bias"], 1)], ALU.mult,
                                          ALU.add).then_inc(ss("sb_zraw" if diag else "sb_zs"), 1)
                        if diag:
                            dve.wait_ge(ss("sb_zraw"), NDIAG * h + (DIAG[u] + 1))
                            tt_(zs[:, 0:P], zs[:, 0:P], lim, ALU.min, ss("sb_zs"))

                    def exponent(u):
                        w = UNITS[u][3]
                        dve.wait_ge(ss("sb_s"), NU * h + (u + 1))
                        if u >= 4 or hh:
                            dve.wait_ge(ss("sb_aa"), NU * h + (u - 3))
                        tt_(sb["ea"][:, u % 4, 0:w], sb["zs"][:, u % 4, 0:w], ps[:, 5, 0:w],
                            ALU.subtract, ss("sb_ea"))

                    def later(u):
                        half, j, q0, w = UNITS[u]
                        cols = slice(q0 - 512 * half, 512)
                        if j == 0:
                            return
                        dve.wait_ge(ss("sb_sp"), NU * h + (u + 1))
                        if j == 4 * half + 3:
                            dve.wait_ge(ss("sb_rr0"), 2 * h + (2 - half))
                            copy(sb["rr"][:, (u + 1) % 2, cols], sb["sp"][:, u % 2, 0:w], ss("sb_rr"))
                        else:
                            dve.wait_ge(ss("sb_rr"), NLATER * h + LATER[u - 1] + 1)
                            tt_(sb["rr"][:, (u + 1) % 2, cols], sb["rr"][:, u % 2, cols],
                                sb["sp"][:, u % 2, 0:w], ALU.add, ss("sb_rr"))

                    def softplus(u):
                        half, j, q0, w = UNITS[u]
                        dve.wait_ge(ss("sb_lg"), NU * h + (u + 1))
                        stt(sb["sp"][:, u % 2, 0:w], sb["zs"][:, u % 4, 0:w], 0.0, sb["lg"][:, u % 4, 0:w],
                            ALU.max, ALU.add, ss("sb_sp"))
                        if j == 4 * half + 3:
                            if u or hh:
                                dve.wait_ge(ss("sb_rr"), NLATER * h + LATER.get(u - 1, LATER.get(u - 2, -1)) + 1)
                            dve.memset(sb["rr"][:, :, :], 0.0).then_inc(ss("sb_rr0"), 1)

                    score(0)
                    score(1)
                    for g in range(NU // 2):
                        if g + 1 < NU // 2:
                            score(2 * g + 2)
                            score(2 * g + 3)
                        softplus(2 * g)
                        later(2 * g)
                        softplus(2 * g + 1)
                        exponent(2 * g)
                        later(2 * g + 1)
                        exponent(2 * g + 1)
                    dve.wait_ge(ss("sb_o"), NU * h + NU)
                    fixed()
                    for half in range(2):
                        copy(C[:, bass.ds(h + H, 1), 512 * half:512 * half + 512],
                             ps[:, 6 + half:7 + half, :], ss("sb_oev"))
                end_stage(dve, end_dve, i + 1)
            dve.wait_ge(ss("ld_rope"), 16)
            dve.memset(rt["st"][:, 0, :], 0.0).then_inc(ss("r_st0"), 1)
            dve.memset(rt["zz"][:, 5:8, :], 0.0).then_inc(ss("r_st0"), 1)

            def head(i):
                hb, z = rt["hb"], rt["zz"]
                fixed()
                copy(hb[:, :], con[:, bass.ds(HB * i + C_HEAD, HB)], ss("r_hb"))
                fixed()
                copy(rt["selp"][:, :, :], sel[:, bass.ds(2 * i, 2), :], ss("r_selp"))
                half_ = P // 2
                dve.wait_ge(ss("r_ev"), 4 * i + 1)
                for n, (name, done) in enumerate((("rq", ss("r_q")), ("rk", ss("r_k")))):
                    x = rt[name]
                    if n:
                        dve.wait_ge(ss("r_q"), i + 1)
                    tt_(rt["t1"][:, :], x[:, :], rt["cs"][:, 0, :], ALU.mult, ss("r_rot"))
                    for a, b in ((0, half_), (half_, 0)):
                        tt_(rt["t2"][a:a + half_, :], x[b:b + half_, :], rt["cs"][b:b + half_, 1, :],
                            ALU.mult, ss("r_rot"))
                    dve.wait_ge(ss("r_rot"), 6 * i + (3 * n + 3))
                    tt_(x[:, :], rt["t1"][:, :], rt["t2"][:, :], ALU.add, done)
                dve.wait_ge(ss("r_k"), i + 1)
                dve.wait_ge(ss("r_hb"), i + 1)
                tt_(rt["qd"][:, :, :], rt["rq"][:, 0:T].rearrange("p (c n) -> p c n", c=TT),
                    hb[:, P:2 * P].unsqueeze(1).broadcast_to((P, TT, P)), ALU.mult, ss("r_qd"))

                def page_scores(m):
                    dve.wait_ge(ss(f"ld_pg{m % 2}"), 256 * i + 32 * (m // 2 + 1))
                    for n in (2 * m, 2 * m + 1):
                        b, g = n // PG, n % PG
                        if n % 2:
                            dve.wait_ge(ss("y_k"), 8 * i + (m + 1))
                        elif m:
                            dve.wait_ge(pg_free, 16 * i + (2 + m))
                        for h in range(H):
                            col = g * 8 + b * 4 + h
                            ins = dve.tensor_tensor_reduce(
                                rt["junk"][:, h * P:(h + 1) * P], rt["pg"][:, m % 2, n % 2, h * P:(h + 1) * P],
                                rt["qb"][:, b, h * P:(h + 1) * P], 1.0, 0.0, ALU.mult, ALU.add,
                                z[:, 0, col:col + 1])
                        ins.then_inc(pg_free if n % 2 else ss("y_k"), 1)

                dve.wait_ge(ss("r_qbc"), i + 1)
                for m in range(4):
                    page_scores(m)
                dve.wait_ge(ss("r_kT"), i + 1)
                for j in range(2):
                    dve.tensor_scalar(rt["kt"][:, 4 * j:4 * j + 4, :], ps[:, 4 + j, :].rearrange(
                        "p (c n) -> p c n", c=4), hb[:, 2 * P:2 * P + 1], None, ALU.mult)\
                        .then_inc(ss("r_kt"), 1)
                dve.tensor_scalar(rt["kvs"][:, 0, :], ps[0:NS, 3, 0:P], SCALE, None, ALU.mult)\
                    .then_inc(ss("r_kvs"), 1)
                copy(rt["kvs"][:, 1, :], ps[0:NS, 3, P:2 * P], ss("r_kvs"))
                dve.wait_ge(ss("r_kvs"), 2 * i + 2)
                tt_(rt["kms"][:, :, :], rt["kvs"][:, 0:1, :].broadcast_to((NS, NS, P)),
                    con[0:NS, C_ID:C_ID + NS].unsqueeze(2).broadcast_to((NS, NS, P)), ALU.mult, ss("r_kms"))
                dve.wait_ge(ss("r_sc"), i + 1)
                for j in range(2):
                    tt_(rt["sm"][:, 4 * j:4 * j + 4, :], ps[:, 6 + j, :].rearrange("p (c n) -> p c n", c=4),
                        hb[:, 0:P].unsqueeze(1).broadcast_to((P, 4, P)), ALU.mult, ss("r_sm"))
                for m in range(4, 8):
                    page_scores(m)
                bias = prm[:, PCOL["sb_bias"]:PCOL["sb_bias"] + H].unsqueeze(1).broadcast_to((P, 16, H))
                dve.wait_ge(pg_free, 16 * i + 10)
                stt(z[:, 1, :].rearrange("p (a h) -> p a h", h=H), z[:, 0, :].rearrange(
                    "p (a h) -> p a h", h=H), SCALE, bias, ALU.mult, ALU.add, ss("y_z"))
                dve.wait_ge(ss("r_up"), i + 1)
                dve.wait_ge(ss("r_st0"), 2)
                for c in range(TT):
                    if c:
                        dve.wait_ge(ss("r_st"), TT * i + c)
                    stt(rt["st"][:, c + 1, :], rt["st"][:, c, :], hb[:, 2 * P + 1:2 * P + 2],
                        ps[:, 4 + c // 4, (c % 4) * P:(c % 4 + 1) * P], ALU.mult, ALU.add, ss("r_st"))
                dve.wait_ge(ss("r_sup"), i + 1)
                dve.wait_ge(ss("ld_s0"), 16 * i + 16)
                for j in range(2):
                    s4 = rt["s0"][:, 4 * j:4 * j + 4, :]
                    stt(s4, s4, hb[:, 2 * P + 2:2 * P + 3], ps[:, 6 + j, :].rearrange(
                        "p (b n) -> p b n", b=4), ALU.mult, ALU.add, ss("r_s1"))
                dve.wait_ge(ss("y_lg"), i + 1)
                stt(z[:, 4, :], z[:, 1, :], 0.0, z[:, 2, :], ALU.max, ALU.add, ss("y_sp"))
                dve.wait_ge(ss("y_sp"), i + 1)
                for g in range(PG - 1, 0, -1):
                    if g < PG - 1:
                        dve.wait_ge(ss("y_r"), 6 * i + (PG - 1 - g))
                    tt_(z[:, 5, 8 * g - 8:8 * g], z[:, 5, 8 * g:8 * g + 8], z[:, 4, 8 * g:8 * g + 8], ALU.add,
                        ss("y_rr") if g == 1 else ss("y_r"))
                dve.wait_ge(ss("y_s"), i + 1)
                tt_(z[:, 3, :], z[:, 1, :], ps[:, 6, 0:64], ALU.subtract, ss("y_ea"))
                dve.wait_ge(ss("r_mu"), i + 1)
                stt(grp(rt["t2"][:, :]), pset(1), -1.0 / P, grp(rt["t1"][:, :]), ALU.mult, ALU.add, ss("r_d"))
                dve.wait_ge(ss("r_rt"), i + 1)
                dve.reciprocal(rt["rst"][:, :], rt["rst"][:, :]).then_inc(ss("r_rc"), 1)
                dve.wait_ge(ss("r_rc"), i + 1)
                stt(rt["t2"][:, :], rt["t2"][:, :], hb[:, 2 * P + 3:2 * P + 4], rt["rst"][:, :], ALU.mult,
                    ALU.mult, ss("r_n"))
                dve.wait_ge(ss("r_n"), i + 1)
                tt_(C[:, bass.ds(i, 1), :], rt["t2"][:, :].unsqueeze(1), rt["rg"][:, :].unsqueeze(1),
                    ALU.mult, ss("r_c"))
                dve.wait_ge(ss("y_ot"), i + 1)
                fixed()
                copy(C[:, H:2 * H, bass.ds(2 * i + T, 2)], ps[:, 6, 0:8].rearrange("p (h b) -> p h b", b=2),
                     None)
                end_stage(dve, end_dve, i + (E_SB + 1))

            with dve.Fori(0, H) as i:
                head(i)
            for c in range(KC):
                dve.wait_ge(ss("c_hi"), c + 1)
                tt_(Hl[:, c, :], C[:, c, :], Hh[:, c, :].bitcast(F32), ALU.subtract, ss("c_lo"))
            for c in range(KC // 2):
                dve.wait_ge(ld_x[c], 32)
            add_to_x(T_OUT, 1)
            end_stage(dve, end_dve, E_OUT)

            def cross(l, e0, nk, t0, freed):
                def mk(c):
                    dve.wait_ge(*of_layer(l, "mw_used", c + 1))
                    copy(cr["mkT"][:, c, :], ps[:, 3 + c % 3, 0:MEM], ss("mk_ev"))

                norm(nk, PCOL["g_cross"] + KC * l, between=mk)
                with dve.Fori(0, 4) as i:
                    for s in range(2):
                        dve.wait_ge(tile_done, 2 * i + (t0 + s + 1))
                        dve.tensor_scalar(cr["qx"][:, bass.ds(2 * i + s, 1), :].rearrange(
                            "p a (g n) -> p (a g) n", g=GRP), pset(s), SCALE_X, None, ALU.mult)\
                            .then_inc(set_free[s], 1)
                end_stage(dve, end_dve, e0 + 1)

                def maxima(u):
                    dve.wait_ge(*of_layer(l, "x_s", u + 1))
                    if u >= 2:
                        dve.wait_ge(*of_layer(l, "x_p", u - 1))
                    b = (u % 2) * 2
                    dve.tensor_reduce(at["mst"][:, u % 2, 0, :], ps[:, b:b + 2, :].rearrange(
                        "p b (t m) -> p (b t) m", t=2), AXX, ALU.max, negate=True).then_inc(ss("x_m"), 1)

                def scaled(u):
                    m = at["mst"]
                    dve.wait_ge(*of_layer(l, "x_e", 4 * u + 4))
                    dve.reciprocal(m[:, u % 2, 2, :], m[:, u % 2, 1, :]).then_inc(ss("x_r"), 1)
                    dve.wait_ge(*of_layer(l, "x_r", u + 1))
                    tt_(at["p"][:, u % 2, :, :], at["p"][:, u % 2, :, :],
                        m[:, u % 2, 2, :].unsqueeze(2).broadcast_to((P, 4, MEM)), ALU.mult, ss("x_p"))

                def turned(u):
                    dve.wait_ge(*of_layer(l, "x_t", u + 1))
                    if u >= 2:
                        dve.wait_ge(*of_layer(l, "x_o", 2 * (u - 1)))
                    copy(at["pT"][:, u % 2, 1, :], ps[:, 5, :], ss("x_pt1"))

                def out(u):
                    hx, half = u // 2, u % 2
                    for dc in range(2):
                        dve.wait_ge(*of_layer(l, "x_oh", 2 * u + dc + 1))
                        cols = slice(512 * half, 512 * half + 512)
                        tt_(Hl[:, 2 * hx + dc, cols], ps[:, 6 + dc, :], Hh[:, 2 * hx + dc, cols].bitcast(F32),
                            ALU.subtract, ss("x_ol"))

                maxima(0)
                for u in range(8):
                    scaled(u)
                    if u + 1 < 8:
                        maxima(u + 1)
                    turned(u)
                    if u:
                        out(u - 1)
                out(7)
                end_stage(dve, end_dve, e0 + 2)
                dve.memset(c3["pm"][:, :, :], 0.0).then_inc(ss("xs_pm"), 1)
                for b in range(NS):
                    dve.wait_ge(*of_layer(l, f"ld_cc_{b % RING}", 16 * (b // RING + 1)))
                    dve.wait_ge(*of_layer(l, "xs_qb", b + 1))
                    if b:
                        dve.wait_ge(*of_layer(l, "cc_used", b))
                    for m in range(MT):
                        for h in range(H):
                            d = slice(h * HDX, (h + 1) * HDX)
                            ins = dve.tensor_tensor_reduce(
                                c3["junk2"][:, m, d], c3["cc"][:, b % RING, m, d],
                                ps[:, 2 * (b % 2) + h // 2, (h % 2) * HDX:(h % 2 + 1) * HDX], 1.0, 0.0,
                                ALU.mult, ALU.add, c3["zc"][:, m, 4 * b + h:4 * b + h + 1])
                    ins.then_inc(ss("cc_used"), 1)
                dve.wait_ge(*of_layer(l, "xs_t", 1))
                z = c3["zst"]
                dve.tensor_reduce(z[:, 0:1], ps[0:32, 4, 0:MEM], AXX, ALU.max, negate=True)\
                    .then_inc(ss("xs_soft"), 1)
                dve.wait_ge(*of_layer(l, "xs_e", 1))
                dve.reciprocal(z[:, 2:3], z[:, 1:2]).then_inc(ss("xs_soft"), 1)
                dve.wait_ge(*of_layer(l, "xs_soft", 2))
                dve.tensor_scalar(c3["pr"][:, :], c3["pr"][:, :], z[:, 2:3], None, ALU.mult)\
                    .then_inc(ss("xs_soft"), 1)
                dve.wait_ge(*of_layer(l, "xs_t", 2))
                dve.wait_ge(*of_layer(l, "xs_pm", 1))
                for m in range(MT):
                    copy(c3["pm"][:, m * H:(m + 1) * H, 0:NS * NS:NS + 1],
                         ps[:, 5, m * 32:(m + 1) * 32].rearrange("p (b h) -> p h b", h=H), ss("xs_soft"))
                dve.wait_ge(*of_layer(l, "xs_oh", 1))
                tt_(Hl[:, :, T:N], ps[:, 4, 0:KC * NS].rearrange("p (c b) -> p c b", c=KC),
                    Hh[:, :, T:N].bitcast(F32), ALU.subtract, None)
                end_stage(dve, end_dve, e0 + 3)
                add_to_x(t0 + 8, nk + 1)
                end_stage(dve, end_dve, e0 + 4)

            def ffn(l, e1, nk, t0, freed):
                dve.memset(ff["ub"][:, :, 0:2], 0.0)
                norm(nk, PCOL["g_ffn"] + KC * l)
                dve.wait_ge(*of_layer(l, "ld_stf", 16))
                fp, ub, cb, gf = ff["fp"], ff["ub"], ff["cb"], ff["gf"]

                def xadd(n, i, t):
                    if n % 4 == 3:
                        dve.wait_ge(tile_done, t + (n // 4 + 1))
                    else:
                        dve.wait_ge(*of_layer(l, "f_dn", 6 * i + (n - n // 4 + 1)))
                    tt_(grp(X[:, n, :]), pset(n % 2), grp(X[:, n, :]), ALU.add, set_free[n % 2])

                def section(i, par, f, between):
                    fixed()
                    copy(fp[:, 0:16], prm[:, bass.ds(16 * i + PCOL[f"ffn{l}"], 16)], None)
                    copy(fp[:, 16:80].rearrange("p (a n) -> p a n", a=1), ff["stf"][:, bass.ds(i, 1), :],
                         ss("f_fp"))
                    dve.wait_ge(*of_layer(l, "f_fp", i + 1))
                    for k in range(2):
                        for v in range(2):
                            q = 2 * k + v
                            c0 = 16 * i + 4 * q
                            dve.wait_ge(set_free[v], f + (k + 2))
                            for tap in range(2):
                                if tap:
                                    dve.wait_ge(*of_layer(l, "f_c", c0 + 1))
                                stt(cb[:, v, 0:T], ub[:, v, tap:tap + T], fp[:, 4 * q + tap:4 * q + tap + 1],
                                    cb[:, v, 0:T], ALU.mult, ALU.add, ss("f_c"))
                                if tap:
                                    dve.wait_ge(*of_layer(l, "f_c", c0 + 2))
                                stt(cb[:, v, T:N], fp[:, 16 + 16 * q + 8 * tap:24 + 16 * q + 8 * tap],
                                    fp[:, 4 * q + tap:4 * q + tap + 1], cb[:, v, T:N], ALU.mult, ALU.add,
                                    ss("f_c"))
                                if q == 3 and tap == 0:
                                    between(0)
                            copy(ff["ftl"][:, 10 * q:10 * q + 10], ub[:, v, T:T + 10], ss("f_ft"))
                        if k:
                            between(1)
                        dve.wait_ge(*of_layer(l, "f_sl", 2 * i + (k + 1)))
                        dve.wait_ge(*of_layer(l, "f_c", 16 * i + (8 * k + 8)))
                        tt_(gf[:, :], cb[:, 0, :], cb[:, 1, :], ALU.mult, ss("f_gm"))
                        if k:
                            between(2)
                        dve.wait_ge(*of_layer(l, "g_hi", 2 * i + (k + 1)))
                        tt_(ff["Gl"][:, par, k, :], gf[:, :], ff["Gh"][:, par, k, :].bitcast(F32),
                            ALU.subtract, ss("g_lo"))
                    dve.wait_ge(*of_layer(l, "f_ft", 4 * i + 4))
                    fixed()
                    copy(ff["tls"][:, bass.ds(i, 1), :], ff["ftl"][:, :].rearrange("p (a n) -> p a n", a=1),
                         ss("f_tl"))
                    for n in range(3, 8):
                        between(n)

                section(0, 0, freed, lambda n: None)
                with dve.Fori(0, SEC // 2) as r:
                    for j in (1, 2):
                        section(2 * r + j, j % 2, 12 * r + (freed + 2 + 6 * (j - 1)),
                                lambda n: xadd(n, 2 * r + (j - 1), 12 * r + (t0 + 8 + 6 * (j - 1))))
                for n in range(8):
                    xadd(n, SEC - 1, t0 + 6 * SEC - 2)
                    if n:
                        sum_square(nk + 1, n - 1)
                sum_square(nk + 1, KC - 1)
                end_stage(dve, end_dve, e1)

            cross(*CR[0])
            ffn(0, E_FF0, 2, T_FFN0, F_FF0)
            uu, us, cvo, ca, cpar = (cf[x] for x in ("uu", "us", "cvo", "ca", "cpar"))
            dve.memset(uu[:, :, 0:W_CONV - 1], 0.0).then_inc(ss("c_ch"), 1)
            norm(3, PCOL["g_mix"] + KC)
            dve.wait_ge(ss("ld_us"), 16)

            def conv_parameters(c, j):
                fixed()
                copy(cpar[:, j:j + 1, :], prm[:, bass.ds(CFP * c + PCOL["cf"], CFP)].rearrange(
                    "p (j n) -> p j n", j=1), ss("c_par"))

            def gate(c, j):
                dve.wait_ge(set_free[1], c + (F_W1 + 2))
                stt(grp(uu[:, j, W_CONV - 1:W_CONV - 1 + N]), pset(0), cpar[:, j, 0:1], grp(cf["sg"][:, :]),
                    ALU.add, ALU.mult, set_free[0])

            def convolve(c, j, more):
                u = uu[:, j, W_CONV - 1:W_CONV - 1 + N]
                dve.wait_ge(ss("c_ch"), 2 * c + 1)
                if more:
                    conv_parameters(c + 1, 1 - j)
                dve.wait_ge(set_free[0], c + (F_W1 + 2))
                dve.tensor_scalar(ca[:, 0:T], uu[:, j, 0:T], cpar[:, j, 3:4], cpar[:, j, 2:3], ALU.mult,
                                  ALU.add).then_inc(ss("c_tap"), 1)
                copy(cf["utl"][:, bass.ds(c, 1), :], uu[:, j, T:T + W_CONV - 1].unsqueeze(1), None)
                copy(us[:, bass.ds(c, 1), :, W_CONV - 1:W_CONV], u[:, T:N].rearrange(
                    "p (a b n) -> p a b n", a=1, n=1), ss("c_u"))
                dve.wait_ge(ss("c_u"), c + 1)
                tt_(cf["usj"][:, :, :].unsqueeze(1), us[:, bass.ds(c, 1), :, :],
                    cpar[:, j, 3:3 + W_CONV].unsqueeze(1).unsqueeze(1).broadcast_to((P, 1, NS, W_CONV)),
                    ALU.mult, ss("c_sm"))
                dve.wait_ge(ss("c_sm"), c + 1)
                dve.tensor_reduce(ca[:, T:N], cf["usj"][:, :, :], AXX, ALU.add).then_inc(ss("c_sr"), 1)
                for w in range(1, W_VE):
                    dve.wait_ge(ss("c_tap"), W_VE * c + w)
                    stt(ca[:, 0:T], uu[:, j, w:w + T], cpar[:, j, 3 + w:4 + w], ca[:, 0:T], ALU.mult,
                        ALU.add, ss("c_tap"))
                dve.wait_ge(ss("c_sr"), c + 1)
                fixed()
                dve.tensor_scalar(cvo[:, bass.ds(c, 1), T:N], ca[:, T:N].unsqueeze(1), cpar[:, j, 2:3],
                                  None, ALU.add).then_inc(ss("c_ch"), 1)
                if more:
                    gate(c + 1, 1 - j)
                dve.wait_ge(ss("c_tap"), W_VE * c + W_VE)
                dve.wait_ge(ss("c_pt"), c + 1)
                tt_(cvo[:, bass.ds(c, 1), 0:T].rearrange("p a (b n) -> p (a b) n", b=2),
                    ca[:, 0:T].rearrange("p (b n) -> p b n", b=2), ps[:, 6:8, :], ALU.add, ss("c_ch"))

            conv_parameters(0, 0)
            dve.wait_ge(ss("c_par"), 1)
            dve.wait_ge(ss("c_ch"), 1)
            gate(0, 0)
            with dve.Fori(0, KC // 2 - 1) as i:
                convolve(2 * i, 0, True)
                convolve(2 * i + 1, 1, True)
            convolve(KC - 2, 0, True)
            convolve(KC - 1, 1, False)
            end_stage(dve, end_dve, E_FF0 + 1)
            dve.wait_ge(ss("l_mu"), 1)
            for c in range(KC):
                stt(grp(cvo[:, c, :]), pset(0), -1.0 / D, grp(cvo[:, c, :]), ALU.mult, ALU.add, ss("l_d"))
            dve.wait_ge(ss("l_rt"), 1)
            dve.reciprocal(ln["lrst"][:, :], ln["lrst"][:, :]).then_inc(ss("l_rc"), 1)
            dve.wait_ge(ss("l_rc"), 1)

            def ln_lo(c):
                dve.wait_ge(ss("l_hi"), c + 1)
                tt_(Hl[:, c, :], ln["lhf"][:, c % 2, :], Hh[:, c, :].bitcast(F32), ALU.subtract, ss("l_lo"))

            for c in range(KC):
                if c >= 2:
                    dve.wait_ge(ss("l_lo"), c - 1)
                stt(ln["lhf"][:, c % 2, :], cvo[:, c, :], prm[:, PCOL["ln_g"] + c:PCOL["ln_g"] + c + 1],
                    ln["lrst"][:, :], ALU.mult, ALU.mult, ss("l_hf"))
                if c:
                    ln_lo(c - 1)
            ln_lo(KC - 1)
            add_to_x(T_W2, 4, PCOL["b2"])
            end_stage(dve, end_dve, E_CF)
            cross(*CR[1])
            ffn(1, E_FF1, 5, T_FFN1, F_FF1)
            norm(6, PCOL["g_final"], split=False)


_OUTS = {
    "y": (P, KC, N), "sbk": (H, P, N), "sbv": (H, P, N), "retp": (H, P, P), "rets": (NS, H, P, P),
    "cvp": (P, KC, W_CONV - 1), "cvs": (P, KC, NS, W_CONV), "ffn0": (P, SEC, 40), "ffn1": (P, SEC, 40),
    "st0": (P, SEC, 64), "st1": (P, SEC, 64), "mk": (2, P, KC, MEM), "mv": (2, P, MT, D),
}


def _features(a):
    return np.ascontiguousarray(a.T.reshape(-1, P, a.shape[0]).transpose(1, 0, 2))


def _tiles(w):
    k, m = w.shape
    return w.reshape(k // P, P, m // P, P).transpose(2, 1, 0, 3).reshape(m // P, P, k)


def _wide(w):
    return w.reshape(4, 2, P, 2, 512).transpose(3, 0, 2, 1, 4).reshape(8, P, 1024)


def _inputs(i):
    w_in = _tiles(i["w_in_ab"][0])
    order = [4 * p + h for h in range(H) for p in (5, 6, 4)] + [4 * p + h for h in range(H) for p in (1, 2, 0, 3)]
    cv1 = _tiles(i["cv_w1"][0])

    def ffn(l):
        up = _tiles(i["ffn_w_up"][l])
        dn = i["ffn_w_down"][l].reshape(SEC, 2, P, 2, 512).transpose(0, 3, 2, 1, 4).reshape(SEC, 2, P, 1024)
        ups = [up[[2 * s, FC + 2 * s, 2 * s + 1, FC + 2 * s + 1]] for s in range(SEC)]
        out = [ups[0]]
        for s in range(1, SEC):
            out += [ups[s], dn[s - 1]]
        return out + [dn[SEC - 1]]

    wts = [w_in[order], _tiles(i["w_out_ab"][0]), _tiles(i["xa_wq"][0]), _tiles(i["xa_wo"][0]), *ffn(0),
           cv1[[j for c in range(KC) for j in (c, KC + c)]], _tiles(i["cv_w2"][0]),
           _tiles(i["xa_wq"][1]), _tiles(i["xa_wo"][1]), *ffn(1)]
    memw = np.concatenate([x for l in range(2) for x in (_tiles(i["xa_wk"][l]), _wide(i["xa_wv"][l]))])

    def cols(a):
        a = np.atleast_2d(a)
        return a.reshape(a.shape[0], -1, P).transpose(2, 0, 1).reshape(P, -1)

    cfp = np.concatenate([i["cv_b1"][0].reshape(2, D), i["cv_dwb"][0][None], i["cv_dw"][0]])
    cfp = cfp.reshape(CFP, KC, P).transpose(2, 1, 0).reshape(P, KC * CFP)

    def section_chunks(a):
        n = a.shape[0]
        return a.reshape(n, 2, SEC, 2, P).transpose(4, 2, 3, 1, 0).reshape(P, SEC, 4, n)

    par = [cols(i["g_mix"]), cols(i["g_cross"]), cols(i["g_ffn"]), cols(i["g_final"]), cols(i["ret_gn_g"]),
           np.broadcast_to(i["sb_bias"], (P, H)), cfp, cols(i["cv_ln_g"]), cols(i["cv_ln_b"]),
           cols(i["cv_b2"])]
    for l in range(2):
        par.append(section_chunks(np.concatenate([i["ffn_dw"][l], i["ffn_dwb"][l][None]])).reshape(P, -1))
    gn = par[4]

    lg = np.log1p(-np.exp2(-5.0 - np.arange(H, dtype=np.float32))).astype(np.float32)
    idx = np.arange(P)
    con = np.zeros((P, NCON), np.float32)
    con[:, C_ID:C_ID + P] = np.eye(P)
    con[:, C_TRI:C_TRI + P] = idx[:, None] >= idx[None, :]
    con[:, C_ONE:C_ONE + P] = 1.0
    con[:, C_LIM:C_LIM + P] = np.where(idx[:, None] < idx[None, :], BIG, -BIG)
    con[:, C_EPS] = EPS
    for h in range(H):
        a = C_HEAD + h * HB
        diff = (idx[None, :] - idx[:, None]).astype(np.float32)
        con[:, a:a + P] = np.where(diff >= 0, np.exp(np.maximum(diff, 0) * lg[h]), 0.0) * SCALE
        con[:, a + P:a + 2 * P] = np.exp((idx + 1).astype(np.float32) * lg[h])[None, :]
        con[:, a + 2 * P] = np.exp((P - 1 - idx).astype(np.float32) * lg[h]) * SCALE
        con[:, a + 2 * P + 1] = np.exp(np.float32(P) * lg[h])
        con[:, a + 2 * P + 2] = np.exp(lg[h])
        con[:, a + 2 * P + 3] = gn[:, h]
    inv = (np.float32(10000.0) ** (-np.arange(64, dtype=np.float32) / np.float32(64))).astype(np.float32)
    pos = np.concatenate([np.arange(T), np.full(NS, PAST)]).astype(np.float32)
    ang = (inv[:, None] * pos[None, :]).astype(np.float32)
    rope = np.stack([np.concatenate([np.cos(ang)] * 2), np.concatenate([np.sin(ang), -np.sin(ang)])], 1)
    selc = np.zeros((NS, NS, P), np.float32)
    selc[np.arange(NS), np.arange(NS)] = 1.0

    def states(l):
        s = i["state_ffn_conv"][l].transpose(1, 0, 2).reshape(2 * NS, 2 * FF)
        return section_chunks(s).reshape(P, SEC, 64)

    return {
        "x": _features(np.concatenate([i["x_prompt"][0], i["x_sample"][:, 0]])),
        "mem": _features(i["mem_prompt"][0]),
        "wts": np.concatenate(wts),
        "memw": memw, "cons": con, "rope": rope.astype(np.float32), "selc": selc,
        "par": np.concatenate(par, 1),
        "stc": i["state_conv"][0].reshape(NS, W_CONV - 1, KC, P).transpose(3, 2, 0, 1),
        "stf0": states(0), "stf1": states(1),
        "stret": i["state_ret"][0].transpose(1, 2, 0, 3),
        "ck": i["cache_sb_k"][0].reshape(NPAGES, P, H * P), "cv": i["cache_sb_v"][0].reshape(NPAGES, P, H * P),
        "cmk": i["cache_mem_k"].reshape(2, NS, MEM, D), "cmv": i["cache_mem_v"].reshape(2, NS, MEM, D),
        "pt": i["page_table"].reshape(1, NS * PG).astype(np.int32),
    }


def _tokens(a):
    return a.transpose(2, 1, 0).reshape(a.shape[2], -1)


def kernel(**inputs):
    from concourse import bacc as _bacc
    from concourse import mybir as _mybir
    from concourse.bass_utils import run_bass_kernel_spmd as _run

    nc = _bacc.Bacc("TRN2", target_bir_lowering=False, num_devices=1)
    arrays, args = {}, []
    for name, a in _inputs({k: np.asarray(v) for k, v in inputs.items()}).items():
        a = np.ascontiguousarray(a)
        arrays[f"in_{name}"] = a
        args.append(nc.dram_tensor(f"in_{name}", a.shape, _mybir.dt.from_np(a.dtype), kind="ExternalInput").ap())
    for name, shape in _OUTS.items():
        args.append(nc.dram_tensor(f"out_{name}", shape, F32, kind="ExternalOutput").ap())
    build(nc, *args)
    r = _run(nc, [arrays], core_ids=[0]).results[0]
    o = {name: np.asarray(r[f"out_{name}"]) for name in _OUTS}

    y = _tokens(o["y"])
    sb = [o[x].transpose(2, 0, 1) for x in ("sbk", "sbv")]

    def taps(l):
        a = o[f"ffn{l}"].reshape(P, SEC, 2, 2, 10)
        return a.transpose(4, 3, 1, 2, 0).reshape(10, 2 * FF)

    def last_state(l):
        a = o[f"st{l}"].reshape(P, SEC, 2, 2, 2, NS)[:, :, :, :, 1]
        return a.transpose(4, 3, 1, 2, 0).reshape(NS, 2 * FF)

    t = [taps(l) for l in range(2)]
    mk = o["mk"].transpose(0, 3, 2, 1).reshape(2, 1, MEM, 4, HDX)
    mv = o["mv"].transpose(0, 2, 1, 3).reshape(2, 1, MEM, 4, HDX)
    out = (
        y[None, :T], y[T:, None],
        sb[0][None, None, :T], sb[1][None, None, :T], sb[0][None, T:, None], sb[1][None, T:, None],
        o["retp"][None, None], o["rets"][None],
        o["cvp"].transpose(2, 1, 0).reshape(1, 1, W_CONV - 1, D),
        o["cvs"][:, :, :, 1:].transpose(2, 3, 1, 0).reshape(1, NS, W_CONV - 1, D),
        np.stack([a[:2] for a in t])[:, None],
        np.stack([np.stack([last_state(l), t[l][2:]], 1) for l in range(2)]),
        mk, mv,
    )
    return tuple(np.ascontiguousarray(a) for a in out)
```
